# Optimizing a Trainium2 kernel written in Bass

```python
import math
import jax
import jax.numpy as jnp
from jax import lax
import numpy as np

D_MODEL = 1024
BATCH = 1
SEQ = 512
DEPTH = 2
DEC_BATCH = 8
DEC_SEQ = 4
PAST_LEN = 2048
PAGE_SIZE = 128

HEAD_DIM = 64
BLK = 128
WIN_STEPS = 128
SWA_HEADS = 16
SWA_KV_HEADS = 2
SWA_WINDOW = WIN_STEPS * 1
SSM_EXPAND = 2
D_INNER = SSM_EXPAND * D_MODEL
SSM_HEAD_DIM = 64
SSM_HEADS = D_INNER // SSM_HEAD_DIM
SSM_GROUPS = 4
D_STATE = 128
CONV_W = 4
CONV_DIM = D_INNER + 2 * SSM_GROUPS * D_STATE
SSD_CHUNK = 128
DIL_PATTERNS = ((128, 1), (512, 4), (2048, 16))
N_DIL = 3
DIL_HEADS = 16
DIL_KV_HEADS = 16
D_FF = 4 * D_MODEL
NORM_EPS = 1e-5
N_EVEN = (DEPTH + 1) // 2
N_ODD = DEPTH // 2

SWA_Q = SWA_HEADS * HEAD_DIM
SWA_KV = SWA_KV_HEADS * HEAD_DIM
EVEN_IN = SWA_Q + 2 * SWA_KV + D_INNER + CONV_DIM + SSM_HEADS
EVEN_MIX = SWA_Q + D_INNER
DIL_Q = DIL_HEADS * HEAD_DIM
DIL_KV = DIL_KV_HEADS * HEAD_DIM
ODD_IN = N_DIL * (DIL_Q + 2 * DIL_KV)

kernel_name = 'hybrid_swa_ssd_dilated_decode_step'

def rmsnorm(x, w):
    xf = x.astype(jnp.float32)
    y = xf * lax.rsqrt(jnp.mean(xf * xf, axis=-1, keepdims=True) + NORM_EPS)
    return (y * w.astype(jnp.float32)).astype(x.dtype)

def alibi_slopes(n):
    return 2.0 ** (-8.0 * jnp.arange(1, n + 1, dtype=jnp.float32) / n)

def softmax_lse(s, sink=None):
    m = jnp.max(s, axis=-1)
    if sink is not None:
        m = jnp.maximum(m, sink)
    e = jnp.exp(s - m[..., None])
    den = jnp.sum(e, axis=-1)
    if sink is not None:
        den = den + jnp.exp(sink - m)
    return e / den[..., None], m + jnp.log(den)

def window_attn_prompt(q, k, v, dil, slopes, sink):
    bsz, s_len, n_kv, n_g, dh = q.shape
    unit = dil * BLK
    s_pad = -(-s_len // unit) * unit
    pad = s_pad - s_len
    n_steps = s_pad // dil
    nb = n_steps // BLK

    def strided(a):
        a = jnp.pad(a, [(0, 0), (0, pad)] + [(0, 0)] * (a.ndim - 2))
        a = a.reshape((bsz, n_steps, dil) + a.shape[2:])
        return jnp.swapaxes(a, 1, 2).reshape((bsz * dil, n_steps) + a.shape[3:])

    def with_prev(a):
        a = a.reshape(bsz * dil, nb, BLK, n_kv, dh)
        prev = jnp.pad(a[:, :-1], [(0, 0), (1, 0), (0, 0), (0, 0), (0, 0)])
        return jnp.concatenate([prev, a], axis=2)

    qb = strided(q).reshape(bsz * dil, nb, BLK, n_kv, n_g, dh)
    kb = with_prev(strided(k))
    vb = with_prev(strided(v))
    scores = jnp.einsum('bnqkgd,bnskd->bnqkgs', qb, kb, preferred_element_type=jnp.float32) * dh ** -0.5
    kpos = jnp.arange(2 * BLK)
    dist = (jnp.arange(BLK)[:, None] + BLK) - kpos[None, :]
    valid = (dist >= 0) & (dist <= WIN_STEPS)
    valid = valid[None] & ((jnp.arange(nb) > 0)[:, None, None] | (kpos >= BLK)[None, None, :])
    bias = -(slopes.reshape(n_kv, n_g)[None, :, :, None]
             * (dist * dil).astype(jnp.float32)[:, None, None, :])
    scores = jnp.where(valid[None, :, :, None, None, :], scores + bias, -jnp.inf)
    p, lse = softmax_lse(scores, sink)
    o = jnp.einsum('bnqkgs,bnskd->bnqkgd', p.astype(v.dtype), vb)

    def unstrided(a):
        a = a.reshape((bsz, dil, n_steps) + a.shape[3:])
        return jnp.swapaxes(a, 1, 2).reshape((bsz, s_pad) + a.shape[3:])[:, :s_len]

    return unstrided(o), unstrided(lse)

def window_attn_sample(q, k_cat, v_cat, n_past, dil, slopes, sink):
    t_len, n_kv, n_g, dh = q.shape[1:]
    steps = jnp.arange(WIN_STEPS + 1)
    idx = n_past + jnp.arange(t_len)[:, None] - dil * steps[None, :]
    valid = idx >= 0
    idx = jnp.maximum(idx, 0)
    kg = k_cat[:, idx]
    vg = v_cat[:, idx]
    scores = jnp.einsum('btkgd,btjkd->btkgj', q, kg, preferred_element_type=jnp.float32) * dh ** -0.5
    bias = -(slopes.reshape(n_kv, n_g)[:, :, None] * (steps * dil).astype(jnp.float32))
    scores = jnp.where(valid[None, :, None, None, :], scores + bias, -jnp.inf)
    p, lse = softmax_lse(scores, sink)
    o = jnp.einsum('btkgj,btjkd->btkgd', p.astype(v_cat.dtype), vg)
    return o, lse

def ssd_scan(x, dt, a, bm, cm, h0):
    bsz, t_len, n_h, p_dim = x.shape
    n_grp, n_st = bm.shape[2:]
    hg = n_h // n_grp
    q_len = min(SSD_CHUNK, t_len)
    t_pad = -(-t_len // q_len) * q_len
    nc = t_pad // q_len
    pad = [(0, 0), (0, t_pad - t_len)]
    x = jnp.pad(x.astype(jnp.float32), pad + [(0, 0), (0, 0)])
    dt = jnp.pad(dt, pad + [(0, 0)])
    bm = jnp.pad(bm.astype(jnp.float32), pad + [(0, 0), (0, 0)]).reshape(bsz, nc, q_len, n_grp, n_st)
    cm = jnp.pad(cm.astype(jnp.float32), pad + [(0, 0), (0, 0)]).reshape(bsz, nc, q_len, n_grp, n_st)
    xdt = (x * dt[..., None]).reshape(bsz, nc, q_len, n_grp, hg, p_dim)
    acum = jnp.cumsum((dt * a).reshape(bsz, nc, q_len, n_grp, hg), axis=2)
    at = jnp.moveaxis(acum, 2, -1)
    causal = jnp.tril(jnp.ones((q_len, q_len), dtype=bool))
    decay = jnp.exp(jnp.where(causal, at[..., :, None] - at[..., None, :], -jnp.inf))
    cb = jnp.einsum('bclgn,bcsgn->bcgls', cm, bm)
    y = jnp.einsum('bcghls,bcsghp->bclghp', cb[:, :, :, None] * decay, xdt)
    to_end = jnp.exp(acum[:, :, -1:] - acum)
    st = jnp.einsum('bclgn,bclghp->bcghpn', bm, xdt * to_end[..., None])

    def step(h, inp):
        da, s_c = inp
        return h * da[..., None, None] + s_c, h

    h_last, h_in = lax.scan(step, h0.astype(jnp.float32).reshape(bsz, n_grp, hg, p_dim, n_st),
                            (jnp.moveaxis(jnp.exp(acum[:, :, -1]), 1, 0), jnp.moveaxis(st, 1, 0)))
    y = y + jnp.einsum('bclgn,cbghpn->bclghp', cm, h_in) * jnp.exp(acum)[..., None]
    y = y.reshape(bsz, t_pad, n_h, p_dim)[:, :t_len]
    return y, h_last.reshape(bsz, n_h, p_dim, n_st)

def ssm_mixer(z, xbc, dt_raw, conv_w, conv_b, dt_bias, a_log, d_skip, norm_w, conv_state, h0):
    bsz, t_len = xbc.shape[:2]
    xpad = jnp.concatenate([conv_state.astype(xbc.dtype), xbc], axis=1)
    conv = conv_b
    for j in range(CONV_W):
        conv = conv + xpad[:, j:j + t_len] * conv_w[j]
    xbc_c = jax.nn.silu(conv)
    nb_ = SSM_GROUPS * D_STATE
    xs = xbc_c[..., :D_INNER].reshape(bsz, t_len, SSM_HEADS, SSM_HEAD_DIM)
    bm = xbc_c[..., D_INNER:D_INNER + nb_].reshape(bsz, t_len, SSM_GROUPS, D_STATE)
    cm = xbc_c[..., D_INNER + nb_:].reshape(bsz, t_len, SSM_GROUPS, D_STATE)
    dt = jax.nn.softplus(dt_raw.astype(jnp.float32) + dt_bias.astype(jnp.float32))
    a = -jnp.exp(a_log.astype(jnp.float32))
    y, h_last = ssd_scan(xs, dt, a, bm, cm, h0)
    y = y + d_skip.astype(jnp.float32)[:, None] * xs.astype(jnp.float32)
    g = y.reshape(bsz, t_len, D_INNER) * jax.nn.silu(z.astype(jnp.float32))
    g = g.reshape(bsz, t_len, SSM_GROUPS, D_INNER // SSM_GROUPS)
    g = g * lax.rsqrt(jnp.mean(g * g, axis=-1, keepdims=True) + NORM_EPS)
    out = (g.reshape(bsz, t_len, D_INNER) * norm_w.astype(jnp.float32)).astype(xbc.dtype)
    return out, xpad[:, -(CONV_W - 1):], h_last

def even_mixer(h, w_in, sinks, conv_w, conv_b, dt_bias, a_log, d_skip, ssm_norm, w_out, past):
    bsz, t_len = h.shape[:2]
    proj = h @ w_in
    o1 = SWA_Q
    o2 = o1 + SWA_KV
    o3 = o2 + SWA_KV
    o4 = o3 + D_INNER
    o5 = o4 + CONV_DIM
    q = proj[..., :o1].reshape(bsz, t_len, SWA_KV_HEADS, SWA_HEADS // SWA_KV_HEADS, HEAD_DIM)
    k = proj[..., o1:o2].reshape(bsz, t_len, SWA_KV_HEADS, HEAD_DIM)
    v = proj[..., o2:o3].reshape(bsz, t_len, SWA_KV_HEADS, HEAD_DIM)
    z = proj[..., o3:o4]
    xbc = proj[..., o4:o5]
    dt_raw = proj[..., o5:]
    slopes = alibi_slopes(SWA_HEADS)
    sink = sinks.astype(jnp.float32).reshape(SWA_KV_HEADS, SWA_HEADS // SWA_KV_HEADS)
    if past is None:
        o_a, _ = window_attn_prompt(q, k, v, 1, slopes, sink)
        n_keep = min(SWA_WINDOW, t_len)
        new_k, new_v = k[:, -n_keep:], v[:, -n_keep:]
        conv_state = jnp.zeros((bsz, CONV_W - 1, CONV_DIM), h.dtype)
        h0 = jnp.zeros((bsz, SSM_HEADS, SSM_HEAD_DIM, D_STATE), jnp.float32)
    else:
        past_k, past_v, conv_state, h0 = past
        n_past = past_k.shape[1]
        k_cat = jnp.concatenate([past_k.astype(k.dtype), k], axis=1)
        v_cat = jnp.concatenate([past_v.astype(v.dtype), v], axis=1)
        o_a, _ = window_attn_sample(q, k_cat, v_cat, n_past, 1, slopes, sink)
        new_k, new_v = k_cat[:, -n_past:], v_cat[:, -n_past:]
    y_ssm, new_conv, new_h = ssm_mixer(z, xbc, dt_raw, conv_w, conv_b, dt_bias, a_log, d_skip,
                                       ssm_norm, conv_state, h0)
    mixed = jnp.concatenate([o_a.reshape(bsz, t_len, SWA_Q).astype(h.dtype), y_ssm], axis=-1)
    return mixed @ w_out, (new_k, new_v, new_conv, new_h)

def odd_mixer(h, w_in, w_out, past):
    bsz, t_len = h.shape[:2]
    proj = h @ w_in
    grp = DIL_HEADS // DIL_KV_HEADS
    q_all = proj[..., :N_DIL * DIL_Q].reshape(bsz, t_len, N_DIL, DIL_KV_HEADS, grp, HEAD_DIM)
    k_all = proj[..., N_DIL * DIL_Q:N_DIL * (DIL_Q + DIL_KV)].reshape(bsz, t_len, N_DIL, DIL_KV_HEADS, HEAD_DIM)
    v_all = proj[..., N_DIL * (DIL_Q + DIL_KV):].reshape(bsz, t_len, N_DIL, DIL_KV_HEADS, HEAD_DIM)
    slopes = alibi_slopes(DIL_HEADS)
    outs, lses, new_state = [], [], []
    for gi, (window, dil) in enumerate(DIL_PATTERNS):
        q, k, v = q_all[:, :, gi], k_all[:, :, gi], v_all[:, :, gi]
        if past is None:
            o, lse = window_attn_prompt(q, k, v, dil, slopes, None)
            n_keep = min(window, t_len)
            new_state += [k[:, -n_keep:], v[:, -n_keep:]]
        else:
            past_k, past_v = past[2 * gi], past[2 * gi + 1]
            n_past = past_k.shape[1]
            k_cat = jnp.concatenate([past_k.astype(k.dtype), k], axis=1)
            v_cat = jnp.concatenate([past_v.astype(v.dtype), v], axis=1)
            o, lse = window_attn_sample(q, k_cat, v_cat, n_past, dil, slopes, None)
            new_state += [k_cat[:, -n_past:], v_cat[:, -n_past:]]
        outs.append(o)
        lses.append(lse)
    wts = jax.nn.softmax(jnp.stack(lses), axis=0)
    o = jnp.sum(wts[..., None] * jnp.stack(outs).astype(jnp.float32), axis=0)
    return o.reshape(bsz, t_len, DIL_Q).astype(h.dtype) @ w_out, tuple(new_state)

def trunk(x, past_even, past_odd, params):
    (norm_mix, norm_mlp, w_up, w_down, final_norm, even_w_in, even_sinks, even_conv_w, even_conv_b,
     even_dt_bias, even_a_log, even_d_skip, even_ssm_norm, even_w_out, odd_w_in, odd_w_out) = params
    new_even, new_odd = [], []
    for layer in range(DEPTH):
        li = layer // 2
        hn = rmsnorm(x, norm_mix[layer])
        if layer % 2 == 0:
            past = None if past_even is None else tuple(s[li] for s in past_even)
            mix, st = even_mixer(hn, even_w_in[li], even_sinks[li], even_conv_w[li], even_conv_b[li],
                                 even_dt_bias[li], even_a_log[li], even_d_skip[li], even_ssm_norm[li],
                                 even_w_out[li], past)
            new_even.append(st)
        else:
            past = None if past_odd is None else tuple(s[li] for s in past_odd)
            mix, st = odd_mixer(hn, odd_w_in[li], odd_w_out[li], past)
            new_odd.append(st)
        x = x + mix
        hn = rmsnorm(x, norm_mlp[layer])
        x = x + jnp.square(jax.nn.relu(hn @ w_up[layer])) @ w_down[layer]
    y = rmsnorm(x, final_norm)
    even_states = tuple(jnp.stack([st[i] for st in new_even]) for i in range(4))
    odd_states = tuple(jnp.stack([st[i] for st in new_odd]) for i in range(2 * N_DIL))
    return y, even_states, odd_states

def setup_inputs(seed: int = 0) -> dict:
    key = jax.random.key(seed)
    ks = jax.random.split(key, 32)

    def nrm(k, shape, scale=1.0):
        return scale * jax.random.normal(k, shape, jnp.float32)

    n_swa = min(SWA_WINDOW, PAST_LEN)
    d0, d1, d2 = [min(w, PAST_LEN) for w, _ in DIL_PATTERNS]
    dt_init = jnp.exp(jax.random.uniform(ks[20], (N_EVEN, SSM_HEADS), jnp.float32,
                                         math.log(1e-3), math.log(1e-1)))
    dt_bias = dt_init + jnp.log(-jnp.expm1(-dt_init))
    a_log = jnp.log(jax.random.uniform(ks[21], (N_EVEN, SSM_HEADS), jnp.float32, 1.0, 16.0))
    return {
        'x_prompt': nrm(ks[0], (BATCH, SEQ, D_MODEL)),
        'x_sample': nrm(ks[1], (DEC_BATCH, DEC_SEQ, D_MODEL)),
        'cache_swa_k': nrm(ks[2], (N_EVEN, DEC_BATCH, n_swa, SWA_KV_HEADS, HEAD_DIM)),
        'cache_swa_v': nrm(ks[3], (N_EVEN, DEC_BATCH, n_swa, SWA_KV_HEADS, HEAD_DIM)),
        'state_conv': nrm(ks[4], (N_EVEN, DEC_BATCH, CONV_W - 1, CONV_DIM)),
        'state_ssm': nrm(ks[5], (N_EVEN, DEC_BATCH, SSM_HEADS, SSM_HEAD_DIM, D_STATE), 0.1),
        'cache_dil0_k': nrm(ks[6], (N_ODD, DEC_BATCH, d0, DIL_KV_HEADS, HEAD_DIM)),
        'cache_dil0_v': nrm(ks[7], (N_ODD, DEC_BATCH, d0, DIL_KV_HEADS, HEAD_DIM)),
        'cache_dil1_k': nrm(ks[8], (N_ODD, DEC_BATCH, d1, DIL_KV_HEADS, HEAD_DIM)),
        'cache_dil1_v': nrm(ks[9], (N_ODD, DEC_BATCH, d1, DIL_KV_HEADS, HEAD_DIM)),
        'cache_dil2_k': nrm(ks[10], (N_ODD, DEC_BATCH, d2, DIL_KV_HEADS, HEAD_DIM)),
        'cache_dil2_v': nrm(ks[11], (N_ODD, DEC_BATCH, d2, DIL_KV_HEADS, HEAD_DIM)),
        'norm_mix': 1.0 + nrm(ks[12], (DEPTH, D_MODEL), 0.02),
        'norm_mlp': 1.0 + nrm(ks[13], (DEPTH, D_MODEL), 0.02),
        'w_up': nrm(ks[14], (DEPTH, D_MODEL, D_FF), D_MODEL ** -0.5),
        'w_down': nrm(ks[15], (DEPTH, D_FF, D_MODEL), D_FF ** -0.5),
        'final_norm': 1.0 + nrm(ks[16], (D_MODEL,), 0.02),
        'even_w_in': nrm(ks[17], (N_EVEN, D_MODEL, EVEN_IN), D_MODEL ** -0.5),
        'even_sinks': nrm(ks[18], (N_EVEN, SWA_HEADS)),
        'even_conv_w': nrm(ks[19], (N_EVEN, CONV_W, CONV_DIM), CONV_W ** -0.5),
        'even_conv_b': nrm(ks[22], (N_EVEN, CONV_DIM), 0.02),
        'even_dt_bias': dt_bias,
        'even_a_log': a_log,
        'even_d_skip': 1.0 + nrm(ks[23], (N_EVEN, SSM_HEADS), 0.02),
        'even_ssm_norm': 1.0 + nrm(ks[24], (N_EVEN, D_INNER), 0.02),
        'even_w_out': nrm(ks[25], (N_EVEN, EVEN_MIX, D_MODEL), EVEN_MIX ** -0.5),
        'odd_w_in': nrm(ks[26], (N_ODD, D_MODEL, ODD_IN), D_MODEL ** -0.5),
        'odd_w_out': nrm(ks[27], (N_ODD, DIL_Q, D_MODEL), DIL_Q ** -0.5),
    }

def reference(x_prompt, x_sample, cache_swa_k, cache_swa_v, state_conv, state_ssm,
              cache_dil0_k, cache_dil0_v, cache_dil1_k, cache_dil1_v, cache_dil2_k, cache_dil2_v,
              norm_mix, norm_mlp, w_up, w_down, final_norm,
              even_w_in, even_sinks, even_conv_w, even_conv_b, even_dt_bias, even_a_log, even_d_skip,
              even_ssm_norm, even_w_out, odd_w_in, odd_w_out):
    params = (norm_mix, norm_mlp, w_up, w_down, final_norm, even_w_in, even_sinks, even_conv_w, even_conv_b,
              even_dt_bias, even_a_log, even_d_skip, even_ssm_norm, even_w_out, odd_w_in, odd_w_out)
    y_prompt, ep, op = trunk(x_prompt, None, None, params)
    y_sample, es, osm = trunk(x_sample, (cache_swa_k, cache_swa_v, state_conv, state_ssm),
                              (cache_dil0_k, cache_dil0_v, cache_dil1_k, cache_dil1_v, cache_dil2_k, cache_dil2_v),
                              params)
    return (y_prompt, y_sample,
            ep[0], es[0], ep[1], es[1], ep[2], es[2], ep[3], es[3],
            op[0], osm[0], op[1], osm[1], op[2], osm[2], op[3], osm[3], op[4], osm[4], op[5], osm[5])


_drawn_inputs = setup_inputs


def setup_inputs(seed=0):
    import zlib

    import numpy as np

    out = dict(_drawn_inputs(seed))
    spreads = {}
    factors = {}
    for name, (base, spread) in spreads.items():
        noise = np.random.default_rng([zlib.crc32(name.encode()), seed]).standard_normal(out[name].shape)
        drawn = base * np.exp(spread * noise) if base else spread * noise
        out[name] = jnp.asarray(drawn.astype(out[name].dtype))
    for name, factor in factors.items():
        out[name] = (out[name] * factor).astype(out[name].dtype)
    return out
```

```python
from contextlib import ExitStack

import numpy as np

import concourse.bass as bass
from concourse import mybir

F32 = mybir.dt.float32
F32R = mybir.dt.float32r
ACT = mybir.ActivationFunctionType
ALU = mybir.AluOpType
AX = mybir.AxisListType

P = 128
D = 1024
SEQ = 512
NB, NT = 8, 4
NS = NB * NT
R = SEQ + NS
HALF = R // 2
KC = D // P
GW = 256
DI = 2048
NH_SSM, HP, NG_SSM, DS = 32, 64, 4, 128
CONV_DIM = DI + 2 * NG_SSM * DS
XC = CONV_DIM // P
CW = 4
DFF = 4096
EVEN_IN = 1024 + 256 + DI + CONV_DIM + NH_SSM
SEG = CW - 1 + NT
CIN = CW - 1 + SEQ + NB * SEG
COUT = CIN - (CW - 1)
EPS = 1e-5
NEG = -1.0e30


class Steps:

    def __init__(self, sem, eng):
        self.sem, self.eng, self.base, self.terms = sem, eng, 0, []

    def mark(self, ins):
        ins.then_inc(self.sem, 1)
        self.base += 1
        return self.value()

    def link(self, ins):
        self.eng.wait_ge(self.sem, self.mark(ins))

    def value(self):
        v = self.base
        for turn, per, _ in self.terms:
            v = turn * per + v
        return v

    def enter(self, turn, per):
        self.terms.append((turn, per, self.base))

    def leave(self):
        _, per, base = self.terms.pop()
        assert self.base - base == per, ("increments per turn", self.base - base)
        self.base = base


CONSTS = [("tri", P, P), ("neg", P, P), ("tri_s", NS, NS), ("neg_s", NS, NS), ("ones_s", NS, NS),
          ("bmask", NS, NB), ("sink", 16, 1), ("dt_bias", 32, 1), ("a_log", 32, 1), ("d_skip", P, 16), ("ssm_norm", P, 16)]
N_CONSTS = sum(w for _, _, w in CONSTS)


AT_CONSTS = [("dist0", 896), ("dist1", P), ("dist2", P), ("slope", 64), ("sdist0", 160), ("sdist1", 160), ("sslope", 16)]
N_AT = sum(w for _, w in AT_CONSTS)


def groups():
    order = [("xbc", 12), ("kv_dt", 2), ("q", 4), ("z", 8)]
    order += [("out0_0", 4), ("out0_1", 4), ("out0_2", 4), ("mlp0", 32)]
    order += [(f"odd_{kind}{g}", 4) for kind in "qkv" for g in range(3)] + [("out1", 4), ("mlp1", 32)]
    first, at = {}, 0
    for name, n in order:
        first[name] = at
        at += n
    return first, dict(order), at


G0, NG, G_END = groups()
DIL = (1, 4, 16)
N_PAST = (128, 512, 2048)
HEAD_DIM = 64


def build(nc, a, o, scratch):
    ctx = ExitStack()
    with ctx:
        def sem(name):
            return ctx.enter_context(nc.semaphore(name))

        def at(name, offset, shape, dt=F32):
            return nc.alloc_sbuf_tensor_at(name=name, shape=shape, dtype=dt, offset=offset)

        ROW = R * 4
        pos = 16640
        x_t = at("x_t", pos, [P, KC, R]); pos += KC * ROW
        A0 = pos
        a_hi = at("a_hi", pos, [P, KC, R], F32R); pos += KC * ROW
        a_lo = at("a_lo", pos, [P, KC, R], F32R); pos += KC * ROW
        B0 = pos
        b_hi = at("b_hi", pos, [P, KC, R], F32R); pos += KC * ROW
        b_lo = at("b_lo", pos, [P, KC, R], F32R); pos += KC * ROW
        w_raw = at("w_raw", pos, [P, 2, KC, GW]); pos += 2 * KC * GW * 4
        w_hi = at("w_hi", pos, [P, 2, KC, GW], F32R); pos += 2 * KC * GW * 4
        w_lo = at("w_lo", pos, [P, 2, KC, GW], F32R); pos += 2 * KC * GW * 4
        norm_w = at("norm_w", pos, [P, 5, KC]); pos += 5 * KC * 4
        rstd = at("rstd", pos, [P, R]); pos += ROW
        S0 = pos
        rstd8 = at("rstd8", pos, [P, R]); pos += ROW
        ssq = at("ssq", pos, [P, R]); pos += ROW
        xw = at("xw", pos, [P, 2, R]); pos += 2 * ROW
        sq = at("sq", pos, [P, 2, R]); pos += 2 * ROW
        ones = at("ones", pos, [P, P]); pos += P * 4
        ident = at("ident", pos, [P, P]); pos += P * 4
        eps_col = at("eps_col", pos, [P, 8]); pos += 32
        U0 = pos
        xbc = at("xbc", pos, [P, XC, R]); pos += XC * ROW
        conv_wb = at("conv_wb", pos, [P, XC, CW + 1]); pos += XC * (CW + 1) * 4
        tails = at("tails", pos, [P, XC, (CW - 1) * (1 + NB)]); pos += XC * 27 * 4
        cin = at("cin", B0, [P, 2, CIN + 1])
        cacc = at("cacc", B0 + 2 * (CIN + 1) * 4, [P, 2, CIN + 1])
        cexp = at("cexp", B0 + 4 * (CIN + 1) * 4, [P, 2, CIN + 1])
        cst = at("cst", B0 + 6 * (CIN + 1) * 4, [P, XC, (CW - 1) * NB])
        o0 = B0 + 6 * (CIN + 1) * 4 + XC * 24 * 4

        def conv_out(t, c):
            return t[:, c, CW - 1 + SEQ:CIN].rearrange("p (b k) -> p b k", b=NB)[:, :, 0:NT]
        stage = at("stage", o0, [P, 4, R])
        o1 = o0 + 4 * ROW
        v_row0 = at("v_row0", o1, [P, 4, P]); o1 += 4 * P * 4
        kv_new0 = at("kv_new0", o1, [NS, 2, P]); o1 += 2 * P * 4
        q_new0 = at("q_new0", o1, [NS, 1024]); o1 += 4096
        dt_raw = at("dt_raw", pos, [32, R]); pos += ROW
        q = A0
        def over_a(name, shape):
            nonlocal q
            t = at(name, q, shape)
            q += -(-int(np.prod(shape[1:])) * 4 // 32) * 32
            return t
        hd_bc = over_a("hd_bc", [P, 2, 8, P])
        decay = over_a("decay", [P, 2, 8, P])
        c_exp = over_a("c_exp", [P, 2, 8, P])
        ssd_x = over_a("ssd_x", [P, 2, 4, P])
        ssd_bc = over_a("ssd_bc", [P, 2, 2, P])
        x_dt = over_a("x_dt", [P, 2, 8, HP])
        assert q <= A0 + 2 * KC * ROW, q - A0
        q = B0
        x_end = over_a("x_end", [P, 2, 8, HP])
        h_t = over_a("h_t", [P, 8, HP])
        hs_t = over_a("hs_t", [P, NB, 8, HP])
        b_row = over_a("b_row", [P, 2, DS])
        b_msk = over_a("b_msk", [NS, NB, DS])
        dt_t = over_a("dt_t", [P, 2, 5, 32])
        a_col = over_a("a_col", [P, 5, 32])
        dte = over_a("dte", [P, 5, 32])
        ea = over_a("ea", [P, 4, 32])
        eas = over_a("eas", [P, NB, 32])
        dta_m = over_a("dta_m", [NS, NB, 32])
        assert q <= B0 + 2 * KC * ROW, q - B0
        dt_w = at("dt_w", S0 + 2 * ROW, [32, 4, R])
        a_row = at("a_row", S0, [32, R])
        q = A0
        at_q = over_a("at_q", [P, 2, R])
        at_k = over_a("at_k", [P, 2, R])
        at_v = over_a("at_v", [P, 2, 4, P])
        at_e = over_a("at_e", [P, 2, 8, P])
        at_pt = over_a("at_pt", [P, 2, 7, P])
        at_c = over_a("at_c", [P, N_AT])
        assert q <= A0 + 2 * KC * ROW, q - A0
        q = A0
        f_bc = over_a("f_bc", [P, 2, 3, R])
        q = B0
        at_st = over_a("at_st", [P, 2, 16])
        at_sr = over_a("at_sr", [16, 2, P])
        sm_st = over_a("sm_st", [P, 2, P])
        sm_q = over_a("sm_q", [P, 2, 2, NS])
        sm_k = over_a("sm_k", [P, 2, 2, NS])
        sm_e = over_a("sm_e", [P, 2, 160])
        sm_ms = over_a("sm_ms", [P, 2, 2])
        sm_pt = over_a("sm_pt", [P, 12, P])
        sm_pn = over_a("sm_pn", [NS, 12, P])
        vn = over_a("vn", [NS, 3 * D])
        assert q <= B0 + 2 * KC * ROW, q - B0
        q = A0 + 6 * ROW
        stt = over_a("stt", [16, 3, 2, R])
        fac = over_a("fac", [16, 3, R])
        assert q <= A0 + 2 * KC * ROW, q - A0
        o_t = [at(f"o_t{g}", U0 + g * KC * ROW, [P, KC, R]) for g in range(3)]
        s0_t = at("s0_t", U0 + XC * ROW + XC * 5 * 4, [P, 16, NS])
        u_q = at("u_q", B0, [P, 2, 16, HEAD_DIM])
        u_p = at("u_p", B0 + 8192, [P, 16, HEAD_DIM])
        u_k = at("u_k", B0 + 12288, [P, 2, P])
        v0s = at("v0s", A0 + 20992, [P, NB, P])
        stage1 = at("stage1", B0, [P, 4, R])
        u1_q = [at("u1_q0", U0 + 32768, [P, NT, D]), at("u1_q1", B0 + 4 * ROW, [P, NT, D])]
        u1_k = at("u1_k", U0, [P, 2, NT, D])
        v_row1 = at("v_row1", B0 + 4 * ROW + 16384, [P, 4, 2 * P])
        row1 = at("row1", B0 + 4 * ROW + 20480, [NS, 2, 2 * P])
        s1_t = at("s1_t", S0 + ROW, [P, 48, NS])
        v1s = at("v1s", A0, [P, 4, D])
        nat = at("nat", A0, [16, 3, 2, R])
        q = pos
        consts = over_a("consts", [P, N_CONSTS]); pos = q
        at_at, cc = {}, 0
        for nm, w in AT_CONSTS:
            at_at[nm] = at_c[:, cc:cc + w]
            cc += w
        c_at = {}
        cc = 0
        for nm, rows, w in CONSTS:
            c_at[nm] = consts[0:rows, cc:cc + w]
            cc += w
        assert pos <= 229344

        gp = ctx.enter_context(nc.psum_tensor("gp", [P, 2, 2, 512], F32))
        mp = ctx.enter_context(nc.psum_tensor("mp", [P, 4, 512], F32))

        w_loaded = [sem("w_loaded0"), sem("w_loaded1")]
        w_hi_done = sem("w_hi_done")
        w_lo_done = sem("w_lo_done")
        mm_done = sem("mm_done")
        drained = sem("drained")
        consts_in = sem("consts_in")
        x_in = sem("x_in")
        eps_set = sem("eps_set")
        ones_set = sem("ones_set")
        v_turned = sem("v_turned")
        q_turned = sem("q_turned")
        rows_out = sem("rows_out")
        acts = sem("acts")
        dves = sem("dves")
        sq_done = sem("sq_done")
        a_w = sem("a_w")
        a_hi_done = sem("a_hi_done")
        a_ready = sem("a_ready")
        ssq_done = sem("ssq_done")
        stat_mm = sem("stat_mm")
        rms_done = sem("rms_done")
        rstd_done = sem("rstd_done")
        b_hi_done = sem("b_hi_done")
        b_ready = sem("b_ready")
        q_row_stored = sem("q_row_stored")
        dt_neg = sem("dt_neg")
        dt_ready = sem("dt_ready")
        atc_in = sem("atc_in")
        at_in = [sem("at_in0"), sem("at_in1")]
        e_pad = sem("e_pad")
        s_mm = sem("s_mm")
        nm_done = sem("nm_done")
        p_done = sem("p_done")
        pt_mm = sem("pt_mm")
        pt_done = sem("pt_done")
        o_mm = sem("o_mm")
        o_done = sem("o_done")
        at_stored = [sem("at_stored0"), sem("at_stored1")]
        uk_in = [sem("uk_in0"), sem("uk_in1")]
        z_in = [sem(f"z_in{c}") for c in range(8)]
        z_silu = sem("z_silu")
        gated = sem("gated")
        gate_sq = sem("gate_sq")
        gate_mm = sem("gate_mm")
        gate_rms = sem("gate_rms")
        y_ready = sem("y_ready")
        dves2 = sem("dves2")
        h_val = sem("h_val")
        uq_in = [sem("uq_in0"), sem("uq_in1")]
        unit_done = sem("unit_done")
        sm_in = [sem("sm_in0"), sem("sm_in1")]
        sms_done = sem("sms_done")
        sms_mm = sem("sms_mm")
        smn_done = sem("smn_done")
        smp_done = sem("smp_done")
        smt_mm = sem("smt_mm")
        smt_done = sem("smt_done")
        sm_stored = [sem("sm_stored0"), sem("sm_stored1")]
        sv_in = [sem("sv_in0"), sem("sv_in1")]
        so_mm = sem("so_mm")
        so_done = sem("so_done")
        vn_in = sem("vn_in")
        stt_in = sem("stt_in")
        fac_done = sem("fac_done")
        fac_act = sem("fac_act")
        fac_stored = sem("fac_stored")
        f_in = [sem("f_in0"), sem("f_in1")]
        merged = sem("merged")
        rows1_mm = sem("rows1_mm")
        rows1_done = sem("rows1_done")
        row_stored = [sem("row_stored0"), sem("row_stored1")]
        v1_mm = sem("v1_mm")
        v1_done = sem("v1_done")
        v1_stored = sem("v1_stored")
        st1 = [sem(f"st1_{i}") for i in range(4)]
        u1_in = [sem("u1_in0"), sem("u1_in1")]
        unit1_done = sem("unit1_done")
        v_in = [sem(f"v_in{i}") for i in range(4)]
        v_used = sem("v_used")
        copied = sem("copied")
        y_out = sem("y_out")
        y_stored = sem("y_stored")
        dt_parts = sem("dt_parts")
        dt_rows = sem("dt_rows")
        a_stored = sem("a_stored")
        a_row_done = sem("a_row_done")
        bc_in = [sem("bc_in0"), sem("bc_in1")]
        hs_in = sem("hs_in")
        hs_out = sem("hs_out")
        h_out = sem("h_out")
        ssd_in = sem("ssd_in")
        cb_mm = sem("cb_mm")
        xr_mm = sem("xr_mm")
        b_row_done = sem("b_row_done")
        b_msk_done = sem("b_msk_done")
        ea_done = sem("ea_done")
        diff_done = sem("diff_done")
        decay_done = sem("decay_done")
        x_dt_done = sem("x_dt_done")
        m_done = sem("m_done")
        c_exp_done = sem("c_exp_done")
        y_mm = sem("y_mm")
        y_done = sem("y_done")
        st_mm = sem("st_mm")
        state_done = sem("state_done")
        conv_sum = sem("conv_sum")
        xbc_ready = sem("xbc_ready")
        st_done = [sem(f"st_done{i}") for i in range(4)]
        out_done = sem("out_done")
        out_hw = sem("out_hw")

        def wait(eng, s, v):
            if isinstance(v, int) and v <= 0:
                return
            eng.wait_ge(s, v)

        AB = {0: 0, "y": 8, 1: 16, 2: 24, 3: 32, 4: 40}
        BB = {"attn0": 0, "y": 8, "mlp0": 16, "attn1": 48, "mlp1": 56}

        def DIST(lay, i):
            return at_at["sdist0" if lay == 0 or i < 2 else "sdist1"]

        def AT_ST(call, C, cc):
            return C * 8 + (64 * call - 8 * cc)

        def turns(eng, n, body, steps=(), peel_first=False, peel_last=False):
            def one(it, last):
                for st, per in steps:
                    st.enter(it, per)
                body(it, last)
                for st, _ in steps:
                    st.leave()
            lo, hi = int(peel_first), (n - 1 if peel_last else n)
            for it in range(lo):
                one(it, False)
            if hi > lo:
                with eng.Fori(lo, hi) as it:
                    one(it, False)
            if peel_last:
                one(n - 1, True)
            for st, per in steps:
                st.base += n * per

        def w_source(ph, it, s):
            if ph == "xbc":
                w, k0, f0 = a["even_w_in"], 0, it * 512 + (1280 + DI + s * GW)
            elif ph == "kv_dt":
                w, k0, f0 = a["even_w_in"], 0, (1024 if s == 0 else EVEN_IN - GW)
            elif ph == "q":
                w, k0, f0 = a["even_w_in"], 0, it * 512 + s * GW
            elif ph == "z":
                w, k0, f0 = a["even_w_in"], 0, it * 512 + (1280 + s * GW)
            elif ph in ("out0_0", "out0_1", "out0_2"):
                w, k0, f0 = a["even_w_out"], int(ph[-1]) * 1024, it * 512 + s * GW
            elif ph == "out1":
                w, k0, f0 = a["odd_w_out"], 0, it * 512 + s * GW
            elif ph.startswith("odd_"):
                w, k0, f0 = a["odd_w_in"], 0, it * 512 + (3072 * "qkv".index(ph[4]) + 1024 * int(ph[5]) + s * GW)
            return w.rearrange("(c p) f -> p c f", p=P)[:, k0 // P:k0 // P + KC, bass.ds(f0, GW)]

        def projection_stored(eng):
            for n in range(4):
                eng.wait_ge(st1[n], 16 * 12)
            for n in range(2):
                eng.wait_ge(row_stored[n], 16 * 18)
            eng.wait_ge(v1_stored, 16 * 12)

        def odd_at(ph):
            return G0[ph] - G0["odd_q0"]

        ODD = [(kind, g) for kind in "qkv" for g in range(3)]
        k1, v1 = o["k1"], o["v1"]

        block = ctx.enter_context(nc.Block())

        @block.sync
        def _(sp):
            sp.dma_start(norm_w[:], a["norm_w"]).then_inc(consts_in, 16)
            sp.dma_start(consts[:], a["consts"]).then_inc(consts_in, 16)
            sp.dma_start(ident[:], a["ident"]).then_inc(consts_in, 16)
            sp.dma_start(conv_wb[:], a["conv_wb"]).then_inc(consts_in, 16)
            sp.dma_start(cst[:], a["conv_state"]).then_inc(consts_in, 16)
            sp.dma_start(x_t[:], a["x_t"]).then_inc(x_in, 16)

            def phase(ph, first=False):
                def body(it, last):
                    for s in range(2):
                        G = G0[ph] + s
                        src = w_source(ph, it, s)
                        wait(sp, w_lo_done, it * 2 + (G - 1))
                        sp.dma_start(w_raw[:, s], src).then_inc(w_loaded[s], 16)
                turns(sp, NG[ph] // 2, body, peel_first=first)

            phase("xbc", True)
            phase("kv_dt")
            phase("q")
            phase("z")

            def load_group(ph, n):
                G = G0[ph] + n
                sp.wait_ge(w_lo_done, G - 1)
                sp.dma_start(w_raw[:, G % 2], w_source(ph, n // 2, n % 2)).then_inc(w_loaded[G % 2], 16)
            load_group("out0_0", 0)

            def ssd_loads():
                sp.wait_ge(a_row_done, 1)
                sp.dma_start(scratch["a_row"], a_row[:]).then_inc(a_stored, 16)
                sp.wait_ge(a_stored, 16)

                def body(g, last):
                    heads = scratch["a_row"][bass.ds(g * 8, 8)]
                    h0 = a["h0"][bass.ds(g, 1)].rearrange("o n b f -> n (o b f)")
                    dsts = [heads[:, c * P:c * P + (P if c < 4 else NS)] for c in range(5)]
                    dsts = [d.rearrange("(o h) l -> o h l", o=1).to_broadcast([P, 8, P if c < 4 else NS])
                            for c, d in enumerate(dsts)]
                    wait(sp, hs_out, g * 16)
                    sp.dma_start(hs_t[:].rearrange("p b h e -> p (b h e)"), h0).then_inc(hs_in, 16)
                    for c in range(5):
                        w = P if c < 4 else NS
                        prev = g * 5 + (0 if c == 0 else c - 1)
                        wait(sp, diff_done, prev)
                        wait(sp, ea_done, prev)
                        sp.dma_start(hd_bc[:, c % 2, :, 0:w], dsts[c]).then_inc(bc_in[c % 2], 16)
                turns(sp, NG_SSM, body, peel_first=True)
            ssd_loads()

            def attention_loads(call):
                lay, g = (0, 0) if call == 0 else (1, call - 1)
                per = 80 if call == 0 else 48
                def body(c2, last):
                    for cc in range(2):
                        if call == 0:
                            kv = (c2 * 2) // 4 if isinstance(c2, int) else None
                        C = c2 * 2 + cc
                        q_src = scratch["q0" if lay == 0 else "q1"][bass.ds(C + 8 * g, 1)].rearrange("o p n -> p (o n)")
                        if lay == 0:
                            k_src = scratch["k0"][bass.ds(kvh[0], HEAD_DIM)]
                            v_src = scratch["v0"].rearrange("(t p) f -> p t f", p=P)[:, :, bass.ds(kvh[0], HEAD_DIM)]
                        else:
                            k_src = k1[bass.ds(C + 8 * g, 1)].rearrange("o p n -> p (o n)")
                            v_src = v1[g].rearrange("(t p) f -> p t f", p=P)[:, :, bass.ds(C * P, P)]
                        wait(sp, o_mm, c2 * 2 + (8 * call + cc - 1))
                        sp.dma_start(at_q[:, cc], q_src).then_inc(at_in[cc], 16)
                        if lay == 0:
                            for half in range(2):
                                hp = slice(half * HEAD_DIM, (half + 1) * HEAD_DIM)
                                sp.dma_start(at_k[hp, cc], k_src).then_inc(at_in[cc], 16)
                                sp.dma_start(at_v[:, cc, :, hp], v_src).then_inc(at_in[cc], 16)
                        else:
                            sp.dma_start(at_k[:, cc], k_src).then_inc(at_in[cc], 16)
                            sp.dma_start(at_v[:, cc], v_src).then_inc(at_in[cc], 16)
                kvh = [0]
                if lay == 0:
                    for kv in range(2):
                        kvh[0] = kv * HEAD_DIM
                        for c2 in range(2 * kv, 2 * kv + 2):
                            body(c2, False)
                else:
                    turns(sp, 4, body)

            sp.wait_ge(y_done, 5 * NG_SSM)
            sp.wait_ge(out_done, 16 * 19)
            sp.dma_start(at_c[:], a["at_c"]).then_inc(atc_in, 16)
            attention_loads(0)

            def sample_loads(lay):
                def body(i, last):
                    for sl in range(2):
                        hb = i * 2 + sl
                        base = 0 if lay == 0 else 4
                        wait(sp, sms_mm, i * 2 + (base + sl - 1))
                        q = scratch["q%d" % lay][bass.ds(i * 4 + 2 * sl, 2)].rearrange("c p n -> p c n")[:, :, SEQ:R]
                        sp.dma_start(sm_q[:, sl], q).then_inc(sm_in[sl], 16)
                        if lay == 0:
                            k = scratch["k0"][(hb // 2) * HEAD_DIM:(hb // 2 + 1) * HEAD_DIM, SEQ:R]
                            sp.dma_start(sm_k[0:HEAD_DIM, sl, 0], k).then_inc(sm_in[sl], 16)
                            sp.dma_start(sm_k[HEAD_DIM:P, sl, 0], k).then_inc(sm_in[sl], 16)
                        else:
                            k = k1[bass.ds(i * 4 + 2 * sl, 2)].rearrange("c p n -> p c n")[:, :, SEQ:R]
                            sp.dma_start(sm_k[:, sl], k).then_inc(sm_in[sl], 16)
                if lay == 0:
                    for i in range(2):
                        body(i, False)
                else:
                    turns(sp, 6, body)
            sample_loads(0)
            sp.wait_ge(pt_done, 16)
            sp.wait_ge(o_mm, 8)
            sp.dma_start(vn[:, 0:P], scratch["vn0"]).then_inc(vn_in, 16)
            sp.dma_start(v0s[:], a["swa_v"].rearrange("b s f -> s b f")).then_inc(vn_in, 16)

            def merge_loads(lay):
                calls = (0,) if lay == 0 else (1, 2, 3)
                sp.wait_ge(so_mm, 1) if lay == 0 else sp.wait_ge(v_used, 72)
                for i in range(2):
                    sp.wait_ge(at_stored[i], 64 * (calls[-1] + 1))
                    sp.wait_ge(sm_stored[i], 64 if lay == 0 else 256)
                for gi, call in enumerate(calls):
                    sp.dma_start(stt[:, gi, :, 0:SEQ],
                                 scratch["stats"][call].rearrange("(h k t) q -> h k (t q)", h=16, k=2)).then_inc(stt_in, 16)
                    for k in range(2):
                        sp.dma_start(stt[:, gi, k, SEQ:R], scratch["stats_s"][k, 16 * call:16 * call + 16]).then_inc(stt_in, 16)
                n = len(calls)
                sp.wait_ge(fac_done, 1 + lay)
                sp.dma_start(scratch["fac"][0:n].rearrange("g h n -> h g n"), fac[:, 0:n]).then_inc(fac_stored, 16)
                sp.wait_ge(fac_stored, 16 * (1 + lay))

                def body(i, last):
                    for sl in range(2):
                        wait(sp, merged, i * 2 + (8 * lay + sl - 1))
                        for gi in range(n):
                            for half in range(2):
                                row = scratch["fac"][gi][bass.ds(i * 4 + 2 * sl + half, 1)]
                                sp.dma_start(f_bc[half * HEAD_DIM:(half + 1) * HEAD_DIM, sl, gi],
                                             row.to_broadcast([HEAD_DIM, R])).then_inc(f_in[sl], 16)
                turns(sp, 4, body, peel_first=(lay == 0))
            merge_loads(0)

            def z_load(C):
                sp.wait_ge(merged, 8)
                wait(sp, gated, C - 7)
                sp.dma_start(xbc[:, 16 + C % 8], scratch["z0"][C]).then_inc(z_in[C % 8], 16)
            for n, chunks in ((1, range(8)), (2, range(8, 12)), (3, range(12, 16))):
                load_group("out0_0", n)
                for C in chunks:
                    z_load(C)
            phase("out0_1")
            phase("out0_2")

            def mlp_loads(lay):
                ph = f"mlp{lay}"
                up, down = a[f"w_up{lay}"], a[f"w_down{lay}"]

                def body(j, last):
                    for part, w in enumerate((up, down)):
                        for i in range(2):
                            for s in range(2):
                                f0 = i * 512 + s * GW
                                if part == 0:
                                    src = w.rearrange("(c p) f -> p c f", p=P)[:, :, bass.ds(j * 1024 + f0, GW)]
                                else:
                                    src = w.rearrange("(k p) f -> p k f", p=P)[:, bass.ds(j * 8, 8), f0:f0 + GW]
                                G = G0[ph] + 4 * part + 2 * i + s
                                wait(sp, w_lo_done, j * 8 + (G - 1))
                                sp.dma_start(w_raw[:, s], src).then_inc(w_loaded[s], 16)
                turns(sp, 4, body)
            mlp_loads(0)
            for kind, g in ODD:
                phase(f"odd_{kind}{g}")
            load_group("out1", 0)

            sp.wait_ge(mm_done, 2 * G0["out1"])
            projection_stored(sp)
            sp.dma_start(at_c[:], a["at_c"]).then_inc(atc_in, 16)
            for call in (1, 2, 3):
                attention_loads(call)
            sample_loads(1)
            sp.wait_ge(o_mm, 32)
            sp.dma_start(vn[:], scratch["rows1"][2]).then_inc(vn_in, 16)
            for g in range(3):
                src = a[f"dil{g}_v"]
                first = (0, 8, 40)[g]

                def body(it, last):
                    for j in range(4):
                        if g == 0:
                            tile = src[bass.ds(it * 4 + j, 1)].rearrange("o s f -> s (o f)")
                        else:
                            tile = src[bass.ds(it, 1)].rearrange("o (i r) f -> i r (o f)", r=DIL[g])[:, j]
                        wait(sp, v_used, it * 4 + (first + j - 3))
                        sp.dma_start(v1s[:, j], tile).then_inc(v_in[j], 16)
                turns(sp, 2 if g == 0 else 8, body, peel_first=(g == 0))
            merge_loads(1)
            for n in range(1, 4):
                load_group("out1", n)
            mlp_loads(1)
            for h in range(4):
                sp.wait_ge(y_out, 2 * h + 2)
                sp.dma_start(o["y"][:, 2 * h:2 * h + 2], x_t[:, 2 * h:2 * h + 2]).then_inc(y_stored, 16)
            sp.wait_ge(y_stored, 64)

        @block.scalar
        def _(act):
            st = Steps(acts, act)

            def split(ph, it, s):
                G, s1 = G0[ph] + s, (s + 1) % 2
                if isinstance(it, int) and it * 2 + G + 1 >= G_END:
                    return
                act.wait_ge(w_loaded[s1], it * 16 + 16 * ((G + 1) // 2 + 1))
                wait(act, mm_done, it * 4 + 2 * G)
                nc.scalar.activation(w_hi[:, s1], w_raw[:, s1], ACT.Copy).then_inc(w_hi_done, 1)

            act.wait_ge(consts_in, 80)
            for c in range(KC):
                act.wait_ge(a_w, c + 1)
                nc.scalar.activation(a_hi[:, c], xw[:, c % 2], ACT.Copy).then_inc(a_hi_done, 1)
                wait(act, ssq_done, c - 1)
                nc.scalar.activation(sq[:, c % 2], x_t[:, c], ACT.Square).then_inc(sq_done, 1)
            act.wait_ge(w_loaded[0], 16)
            nc.scalar.activation(w_hi[:, 0], w_raw[:, 0], ACT.Copy).then_inc(w_hi_done, 1)

            def rms(i):
                act.wait_ge(stat_mm, i + 1)
                act.wait_ge(eps_set, 1)
                nc.scalar.activation(rstd[:].rearrange("p (h n) -> p h n", h=2), mp[:, 0:2, 0:HALF], ACT.Sqrt,
                                     bias=eps_col[:, 0:1], scale=1.0 / D).then_inc(rms_done, 1)
            rms(0)

            def keep(nm, b, r0, n):
                act.dma_start(o[nm + "s"][bass.ds(b, 1), r0:r0 + n], a[nm][bass.ds(b, 1), r0 + NT:r0 + NT + n]).then_inc(copied, 16)
            for nm in ("swa_k", "swa_v", "dil0_k", "dil0_v"):
                act.dma_start(o[nm + "s"][:, 0:P - NT], a[nm][:, NT:P]).then_inc(copied, 16)

            def body(it, last):
                for s in range(2):
                    split("xbc", it, s)
                    for c in range(2):
                        n = 2 * s + c
                        seqs = cin[:, c, CW - 1 + SEQ:CIN].rearrange("p (b k) -> p b k", b=NB)
                        wait(act, conv_sum, it * 4 + (n - 1))
                        act.wait_ge(consts_in, 80)
                        st.mark(nc.scalar.activation(
                            seqs[:, :, 0:CW - 1],
                            cst[:, bass.ds(it * 4 + n, 1), :].rearrange("p o (b k) -> p (o b) k", b=NB), ACT.Copy))
                        act.wait_ge(drained, it * 4 + (n + 1))
                        act.wait_ge(consts_in, 80)
                        st.mark(nc.scalar.activation(tails[:, bass.ds(it * 4 + n, 1), 0:CW - 1],
                                                     cin[:, c, SEQ:SEQ + CW - 1].rearrange("p (o k) -> p o k", o=1),
                                                     ACT.Copy))
                        st.mark(nc.scalar.activation(
                            tails[:, bass.ds(it * 4 + n, 1), CW - 1:27].rearrange("p o (b k) -> p (o b) k", b=NB),
                            seqs[:, :, NT:SEG], ACT.Copy))
                        act.wait_ge(conv_sum, it * 4 + (n + 1))
                        act.wait_ge(consts_in, 80)
                        st.mark(nc.scalar.activation(xbc[:, bass.ds(it * 4 + n, 1), 0:SEQ].rearrange("p o n -> p (o n)"),
                                                     cacc[:, c, 0:SEQ], ACT.Silu))
                        nc.scalar.activation(
                            xbc[:, bass.ds(it * 4 + n, 1), SEQ:R].rearrange("p o (b k) -> p (o b) k", b=NB),
                            conv_out(cacc, c), ACT.Silu).then_inc(xbc_ready, 1)
            turns(act, NG["xbc"] // 2, body, [(st, 16)], peel_first=True)
            act.wait_ge(acts, st.value())
            act.dma_start(o["conv"], tails[:]).then_inc(out_hw, 16)

            def plain(ph):
                def body(it, last):
                    for s in range(2):
                        split(ph, it, s)
                        if ph == "z":
                            keep("dil1_k", it * 2 + s, 0, 508)
                turns(act, NG[ph] // 2, body)
            plain("kv_dt")
            plain("q")
            plain("z")

            act.wait_ge(dt_neg, 1)
            nc.scalar.activation(dt_w[:, 1], dt_w[:, 1], ACT.Exp).then_inc(dt_parts, 1)
            nc.scalar.activation(eps_col[0:32, 1:2], c_at["a_log"], ACT.Exp).then_inc(dt_parts, 1)
            act.wait_ge(dt_rows, 2)
            nc.scalar.activation(ea[:], mp[:, 1, 160:288].rearrange("p (c h) -> p c h", c=4), ACT.Exp)
            nc.scalar.activation(eas[:], mp[:, 3, 32:288].rearrange("p (c h) -> p c h", c=NB), ACT.Exp).then_inc(dt_parts, 1)
            act.wait_ge(dt_neg, 2)
            nc.scalar.activation(dte[:, 0:4], dte[:, 0:4], ACT.Exp)
            nc.scalar.activation(dte[0:NS, 4], dte[0:NS, 4], ACT.Exp).then_inc(dt_parts, 1)

            def ssd(g, last):
                for c in range(5):
                    sl, w = c % 2, (P if c < 4 else NS)
                    prev = g * 5 + (0 if c == 0 else c - 1)
                    T = g * 5 + (c + 1)
                    act.wait_ge(bc_in[sl], g * (48 if sl == 0 else 32) + 16 * (c // 2 + 1))
                    wait(act, y_mm, prev)
                    nc.scalar.activation(c_exp[:, sl, :, 0:w], hd_bc[:, sl, :, 0:w], ACT.Exp).then_inc(ea_done, 1)
                    act.wait_ge(cb_mm, T)
                    wait(act, st_mm, g * 12 + (0 if c == 0 else c - 1))
                    nc.scalar.activation(b_row[0:w, sl], mp[0:w, 0, P:2 * P], ACT.Copy).then_inc(b_row_done, 1)
                    act.wait_ge(diff_done, T)
                    nc.scalar.activation(decay[0:w, sl, :, 0:w], decay[0:w, sl, :, 0:w], ACT.Exp).then_inc(decay_done, 1)
            turns(act, NG_SSM, ssd, peel_first=True)

            def exps(call, c2, cc, half):
                I = 16 * call + 2 * cc + half
                act.wait_ge(nm_done, c2 * 4 + (I + 1))
                wide = call in (0, 1)
                for t in range(4):
                    if wide:
                        e = at_e[:, half, 2 * t + (t == 0):2 * t + 2, :].rearrange("p a b -> p (a b)")
                    else:
                        e = at_e[:, half, t, :]
                    z = nc.scalar.activation(e, e, ACT.Exp, bias=at_st[:, cc, half * 8 + t:half * 8 + t + 1],
                                             accum_out=at_st[:, cc, half * 8 + 4 + t:half * 8 + 5 + t])
                z.then_inc(p_done, 1)

            def o_out(call, C, cc):
                g = 0 if call == 0 else call - 1
                act.wait_ge(o_mm, C + (8 * call + 1))
                act.wait_ge(consts_in, 80)
                dst = (xbc[:, 16:24] if call == 0 else o_t[g][:])[:, bass.ds(C, 1), 0:SEQ]
                nc.scalar.activation(dst.rearrange("p o n -> p (o n)"), mp[:, 2, :], ACT.Copy)
                wait(act, at_stored[cc], AT_ST(call, C, cc))
                nc.scalar.activation(at_sr[:, cc], mp[0:16, 3, 0:P], ACT.Copy).then_inc(o_done, 1)

            def attention(call):
                def body(c2, last):
                    for cc in range(2):
                        for half in range(2):
                            exps(call, c2, cc, half)
                            if half == 0:
                                if isinstance(c2, int) and c2 == 0 and cc == 0:
                                    continue
                                o_out(call, c2 * 2 + (cc - 1), 1 - cc)
                turns(act, 4, body, peel_first=2 if call == 0 else 1)
                o_out(call, 7, 1)
            attention(0)

            def samples(lay):
                hb0 = 0 if lay == 0 else 4
                src = s0_t if lay == 0 else s1_t

                def body(i, last):
                    for sl in range(2):
                        hb = hb0 + sl
                        wait(act, sms_mm, i * 2 + (hb - 1))
                        act.wait_ge(consts_in, 80)
                        nc.scalar.activation(sm_st[:, sl], src[:, bass.ds(i * 8 + sl * 4, 4)].rearrange("p h n -> p (h n)"),
                                             ACT.Copy).then_inc(sms_done, 1)
                        act.wait_ge(smn_done, i * 2 + (hb + 1))
                        nc.scalar.activation(sm_e[:, sl], sm_e[:, sl], ACT.Exp, bias=sm_ms[:, sl, 0:1],
                                             accum_out=sm_ms[:, sl, 1:2]).then_inc(smp_done, 1)
                        act.wait_ge(smt_mm, i * 2 + (hb + 1))
                        act.wait_ge(consts_in, 80)
                        nc.scalar.activation(sm_pt[:, bass.ds(i * 2 + sl, 1)].rearrange("p o n -> p (o n)"),
                                             mp[:, 2 + sl, 160:288], ACT.Copy)
                        nc.scalar.activation(sm_pn[:, bass.ds(i * 2 + sl, 1)].rearrange("p o n -> p (o n)"),
                                             mp[0:NS, 2 + sl, 288:416], ACT.Copy).then_inc(smt_done, 1)
                turns(act, 2 if lay == 0 else 6, body, peel_first=(lay == 0))
            act.wait_ge(unit_done, NS)
            samples(0)

            act.wait_ge(dves2, 2)
            nc.scalar.activation(fac[:, 0], fac[:, 0], ACT.Exp)
            nc.scalar.activation(fac[:, 2], fac[:, 1], ACT.Exp, bias=c_at["sink"]).then_inc(fac_act, 1)

            def hi_of_merged(lay):
                def body(i, last):
                    for sl in range(2):
                        act.wait_ge(merged, i * 2 + (8 * lay + sl + 1))
                        act.wait_ge(consts_in, 80)
                        nc.scalar.activation(b_hi[:, bass.ds(i * 2 + sl, 1)].rearrange("p o n -> p (o n)"), xw[:, sl],
                                             ACT.Copy).then_inc(b_hi_done, 1)
                turns(act, 4, body)
            hi_of_merged(0)

            def split_n(G):
                if G >= G_END:
                    return
                act.wait_ge(w_loaded[G % 2], 16 * (G // 2 + 1))
                act.wait_ge(mm_done, 2 * (G - 1))
                nc.scalar.activation(w_hi[:, G % 2], w_raw[:, G % 2], ACT.Copy).then_inc(w_hi_done, 1)
            for g in range(4):
                split_n(G0["out0_0"] + g + 1)
                for j in range(4):
                    C = 4 * g + j
                    zc = xbc[:, 16 + C % 8]
                    act.wait_ge(z_in[C % 8], 16 * (C // 8 + 1))
                    nc.scalar.activation(zc, zc, ACT.Silu).then_inc(z_silu, 1)
                for j in range(4):
                    C = 4 * g + j
                    act.wait_ge(gated, C + 1)
                    wait(act, gate_mm, C - 1)
                    nc.scalar.activation(sq[:, C % 2], xbc[:, C], ACT.Square).then_inc(gate_sq, 1)
                act.wait_ge(gate_mm, 4 * g + 4)
                wait(act, y_ready, 4 * g)
                nc.scalar.activation(rstd8[:].rearrange("p (h n) -> p h n", h=2), mp[:, 0:2, 0:HALF], ACT.Sqrt,
                                     bias=eps_col[:, 0:1], scale=1.0 / 512).then_inc(gate_rms, 1)
                if g < 2:
                    for j in range(4):
                        C = 4 * g + j
                        act.wait_ge(y_ready, C + 1)
                        nc.scalar.activation(a_hi[:, C], xbc[:, C], ACT.Copy).then_inc(a_hi_done, 1)

            def body(it, last):
                for s in range(2):
                    split("out0_1", it, s)
                    for c in range(2):
                        act.wait_ge(mm_done, 2 * G0["out0_1"])
                        act.wait_ge(y_ready, 16)
                        nc.scalar.activation(b_hi[:, bass.ds(it * 4 + 2 * s + c, 1)],
                                             xbc[:, bass.ds(it * 4 + (8 + 2 * s + c), 1)], ACT.Copy).then_inc(b_hi_done, 1)
            turns(act, 2, body)

            def final_parts(i, it, n):
                if i < 4:
                    act.wait_ge(a_w, it * 4 + (8 * i + n + 1))
                    act.wait_ge(consts_in, 80)
                    nc.scalar.activation(a_hi[:, bass.ds(it * 4 + n, 1)].rearrange("p o n -> p (o n)"), xw[:, n % 2],
                                         ACT.Copy).then_inc(a_hi_done, 1)
                else:
                    act.wait_ge(drained, 2 * (G_END - 4) + n + 1)
                act.wait_ge(ssq_done, it * 4 + (8 * i + n - 1))
                act.wait_ge(consts_in, 80)
                nc.scalar.activation(sq[:, n % 2], x_t[:, bass.ds(it * 4 + n, 1)].rearrange("p o n -> p (o n)"),
                                     ACT.Square).then_inc(sq_done, 1)

            def body(it, last):
                for s in range(2):
                    split("out0_2", it, s)
                    for c in range(2):
                        final_parts(1, it, 2 * s + c)
            turns(act, 2, body)
            rms(1)

            def mlp(lay, i_norm):
                ph = f"mlp{lay}"
                kept = ("dil2_k", "dil2_v")[lay]

                def one(j, G):
                    G += G0[ph]
                    if isinstance(j, int) and 8 * j + G + 1 >= G_END:
                        return
                    s1 = (G + 1) % 2
                    act.wait_ge(w_loaded[s1], j * 64 + 16 * ((G + 1) // 2 + 1))
                    act.wait_ge(mm_done, j * 16 + 2 * G)
                    nc.scalar.activation(w_hi[:, s1], w_raw[:, s1], ACT.Copy).then_inc(w_hi_done, 1)

                def body(j, last):
                    for i in range(4):
                        one(j, i)
                        keep(kept, j * 2, 511 * i, 511)
                        for c in range(2):
                            n = 2 * i + c
                            act.wait_ge(h_val, j * 8 + (32 * lay + n + 1))
                            nc.scalar.activation(b_hi[:, n], xw[:, c], ACT.Copy).then_inc(b_hi_done, 1)
                    for i in range(4):
                        one(j, 4 + i)
                        keep(kept, j * 2 + 1, 511 * i, 511)
                        if last:
                            for c in range(2):
                                final_parts(i_norm, 0, 2 * i + c)
                turns(act, 4, body, peel_last=True)
            mlp(0, 2)
            rms(2)

            def odd(kind, g):
                ph = f"odd_{kind}{g}"
                W = odd_at(ph)

                def body(it, last):
                    for s in range(2):
                        split(ph, it, s)
                        if kind == "q" and g < 2:
                            keep("dil1_v", it * 2 + (4 * g + s), 0, 508)
                        act.wait_ge(rows1_mm, it * 2 + (W + s + 1))
                        wait(act, row_stored[s], it * 16 + 8 * W)
                        nc.scalar.activation(row1[:, s], mp[0:NS, 3, 0:2 * P], ACT.Copy).then_inc(rows1_done, 1)
                        if kind == "v":
                            act.wait_ge(v1_mm, it * 2 + (4 * g + s + 1))
                            wait(act, v1_stored, it * 32 + 16 * (4 * g + s))
                            for c in range(2):
                                z = nc.scalar.activation(v_row1[:, :, c * P:(c + 1) * P],
                                                         mp[:, c, :].rearrange("p (t f) -> p t f", t=4), ACT.Copy)
                            z.then_inc(v1_done, 1)
                turns(act, 2, body, peel_first=(ph == "odd_q0" or ph == "odd_v0"))
            for kind, g in ODD:
                odd(kind, g)

            projection_stored(act)
            act.wait_ge(unit1_done, 24)
            for call in (1, 2, 3):
                attention(call)
            samples(1)
            act.wait_ge(dves2, 3)
            nc.scalar.activation(fac[:], fac[:], ACT.Exp).then_inc(fac_act, 1)
            hi_of_merged(1)

            def body(it, last):
                for s in range(2):
                    split("out1", it, s)
                    for c in range(2):
                        final_parts(3, it, 2 * s + c)
            turns(act, 2, body)
            rms(3)
            mlp(1, 4)
            rms(4)
            act.wait_ge(copied, 16 * (4 + 8 + 8 + 64))

        @block.vector
        def _(dve):
            st = Steps(dves, dve)
            nc.vector.memset(eps_col[:], EPS).then_inc(eps_set, 1)
            nc.vector.memset(ones[:], 1.0).then_inc(ones_set, 1)
            for s in range(2):
                z = nc.vector.memset(cin[:, s, 0:CW - 1], 0.0)
                st.mark(z)

            def split(ph, it, s):
                G, s1 = G0[ph] + s, (s + 1) % 2
                if isinstance(it, int) and it * 2 + G + 1 >= G_END:
                    return
                dve.wait_ge(w_hi_done, it * 2 + (G + 2))
                nc.vector.tensor_tensor(w_lo[:, s1], w_raw[:, s1], w_hi[:, s1].bitcast(F32),
                                        ALU.subtract).then_inc(w_lo_done, 1)

            dve.wait_ge(x_in, 16)
            dve.wait_ge(consts_in, 80)
            for c in range(KC):
                wait(dve, a_hi_done, c - 1)
                nc.vector.tensor_scalar(xw[:, c % 2], x_t[:, c], norm_w[:, 0, c:c + 1], None,
                                        ALU.mult).then_inc(a_w, 1)
                dve.wait_ge(a_hi_done, c + 1)
                nc.vector.tensor_tensor(a_lo[:, c], xw[:, c % 2], a_hi[:, c].bitcast(F32),
                                        ALU.subtract).then_inc(a_ready, 1)
                dve.wait_ge(sq_done, c + 1)
                if c == 0:
                    nc.vector.tensor_copy(ssq[:], sq[:, 0]).then_inc(ssq_done, 1)
                else:
                    dve.wait_ge(ssq_done, c)
                    nc.vector.tensor_tensor(ssq[:], ssq[:], sq[:, c % 2], ALU.add).then_inc(ssq_done, 1)
            dve.wait_ge(w_hi_done, 1)
            nc.vector.tensor_tensor(w_lo[:, 0], w_raw[:, 0], w_hi[:, 0].bitcast(F32),
                                    ALU.subtract).then_inc(w_lo_done, 1)

            def inverse_rms(i):
                dve.wait_ge(rms_done, i + 1)
                st.link(nc.vector.reciprocal(rstd[:], rstd[:]))
                st.link(nc.vector.tensor_scalar(rstd8[:], rstd[:], HEAD_DIM ** -0.5, None, ALU.mult))
            inverse_rms(0)

            def body(it, last):
                for s in range(2):
                    split("xbc", it, s)
                    for c in range(2):
                        n = 2 * s + c
                        dve.wait_ge(mm_done, it * 4 + (n + 1))
                        if not (isinstance(it, int) and n < 2):
                            dve.wait_ge(xbc_ready, it * 4 + (n - 1))
                        nc.vector.tensor_tensor(cin[:, c, CW - 1:CW - 1 + HALF], gp[:, c, 0, 0:HALF],
                                                rstd[:, 0:HALF], ALU.mult)
                        nc.vector.tensor_tensor(cin[:, c, CW - 1 + HALF:CW - 1 + SEQ], gp[:, c, 1, 0:SEQ - HALF],
                                                rstd[:, HALF:SEQ], ALU.mult)
                        nc.vector.tensor_tensor(
                            cin[:, c, CW - 1 + SEQ:CIN].rearrange("p (b k) -> p b k", b=NB)[:, :, CW - 1:SEG],
                            gp[:, c, 1, SEQ - HALF:HALF].rearrange("p (b k) -> p b k", b=NB),
                            rstd[:, SEQ:R].rearrange("p (b k) -> p b k", b=NB), ALU.mult).then_inc(drained, 1)
                        dve.wait_ge(drained, it * 4 + (n + 1))
                        dve.wait_ge(acts, it * 16 + (4 * n + 1))
                        wb = conv_wb[:, bass.ds(it * 4 + n, 1), :]
                        st.link(nc.vector.tensor_scalar(cacc[:, c, 0:COUT], cin[:, c, 0:COUT], wb[:, 0, 0:1], wb[:, 0, 4:5],
                                                        ALU.mult, ALU.add))
                        for j in range(1, CW):
                            ins = nc.vector.scalar_tensor_tensor(out=cacc[:, c, 0:COUT], in0=cin[:, c, j:j + COUT],
                                                                 scalar=wb[:, 0, j:j + 1], in1=cacc[:, c, 0:COUT],
                                                                 op0=ALU.mult, op1=ALU.add)
                            if j < CW - 1:
                                st.link(ins)
                            else:
                                ins.then_inc(conv_sum, 1)
            turns(dve, NG["xbc"] // 2, body, [(st, 12)], peel_first=True)

            E_ = G0["kv_dt"]
            split("kv_dt", 0, 0)
            for c in range(2):
                dve.wait_ge(mm_done, 2 * E_ + c + 1)
                if c == 0:
                    dve.wait_ge(xbc_ready, XC)
                nc.vector.tensor_tensor(stage[:, c].rearrange("p (h n) -> p h n", h=2), gp[:, c, :, 0:HALF],
                                        rstd[:].rearrange("p (h n) -> p h n", h=2), ALU.mult).then_inc(drained, 1)
            dve.wait_ge(v_turned, 1)
            nc.vector.tensor_copy(v_row0[:], mp[:, 2, :].rearrange("p (t f) -> p t f", t=4)).then_inc(rows_out, 1)
            nc.vector.tensor_copy(kv_new0[:], mp[0:NS, 3, 0:2 * P].rearrange("p (t f) -> p t f", t=2)).then_inc(rows_out, 1)
            split("kv_dt", 0, 1)
            dve.wait_ge(mm_done, 2 * E_ + 3)
            nc.vector.nop().then_inc(drained, 1)
            dve.wait_ge(mm_done, 2 * E_ + 4)
            nc.vector.tensor_tensor(dt_raw[:].rearrange("p (h n) -> p h n", h=2), gp[96:128, 1, :, 0:HALF],
                                    rstd[96:128].rearrange("p (h n) -> p h n", h=2), ALU.mult).then_inc(drained, 1)

            def to_stage(ph, scale, base_slot_use):
                def body(it, last):
                    for s in range(2):
                        split(ph, it, s)
                        for c in range(2):
                            n = 2 * s + c
                            dve.wait_ge(mm_done, it * 4 + (2 * G0[ph] + n + 1))
                            wait(dve, st_done[n], it * 16 + 16 * base_slot_use[n])
                            nc.vector.tensor_tensor(stage[:, n].rearrange("p (h n) -> p h n", h=2), gp[:, c, :, 0:HALF],
                                                    scale[:].rearrange("p (h n) -> p h n", h=2),
                                                    ALU.mult).then_inc(drained, 1)
                        if ph == "z":
                            if isinstance(it, int) and it == 0 and s == 0:
                                dve.wait_ge(out_hw, 16)
                            for t in range(NT):
                                sl = t % 2
                                dve.wait_ge(uk_in[s], it * 16 + 16)
                                dve.wait_ge(uq_in[sl], it * 64 + (32 * s + 16 * (t // 2) + 16))
                                wait(dve, unit_done, it * 8 + (4 * s + t))
                                for kv in range(2):
                                    k = u_k[:, s:s + 1, kv * HEAD_DIM:(kv + 1) * HEAD_DIM].to_broadcast([P, 8, HEAD_DIM])
                                    z = nc.vector.tensor_tensor(u_p[:, 8 * kv:8 * kv + 8], u_q[:, sl, 8 * kv:8 * kv + 8],
                                                                k, ALU.mult)
                                st.link(z)
                                nc.vector.tensor_reduce(s0_t[:, :, bass.ds(it * 8 + (4 * s + t), 1)], u_p[:], AX.X,
                                                        ALU.add).then_inc(unit_done, 1)
                        if ph == "q":
                            dve.wait_ge(q_turned, it * 2 + (s + 1))
                            nc.vector.tensor_scalar(
                                q_new0[:, bass.ds(it * 512 + s * 256, 256)], mp[0:NS, 3, 0:2 * P], 1.0, None,
                                ALU.mult).then_inc(rows_out, 1)
                turns(dve, NG[ph] // 2, body, [(st, 8)] if ph == "z" else (), peel_first=True)
            to_stage("q", rstd8, [2, 0, 0, 0])
            to_stage("z", rstd, [4, 2, 2, 2])

            x_, e_, s_, p_ = (dt_w[:, j] for j in range(4))
            st.link(nc.vector.tensor_scalar(x_, dt_raw[:], c_at["dt_bias"], None, ALU.add))
            nc.vector.scalar_tensor_tensor(out=e_, in0=x_, scalar=-1.0, in1=x_, op0=ALU.mult, op1=ALU.min).then_inc(dt_neg, 1)
            dve.wait_ge(dt_parts, 1)
            st.link(nc.vector.tensor_scalar(s_, e_, 2.0, None, ALU.add))
            st.link(nc.vector.reciprocal(s_, s_))
            st.link(nc.vector.tensor_tensor(s_, s_, e_, ALU.mult))
            st.link(nc.vector.tensor_tensor(e_, s_, s_, ALU.mult))
            st.link(nc.vector.tensor_scalar(p_, e_, 1.0 / 15, None, ALU.mult))
            for k in (13, 11, 9, 7, 5, 3):
                st.link(nc.vector.scalar_tensor_tensor(out=p_, in0=p_, scalar=1.0 / k, in1=e_, op0=ALU.add, op1=ALU.mult))
            st.link(nc.vector.scalar_tensor_tensor(out=p_, in0=p_, scalar=1.0, in1=s_, op0=ALU.add, op1=ALU.mult))
            st.link(nc.vector.tensor_scalar(x_, x_, 0.0, None, ALU.max))
            st.link(nc.vector.scalar_tensor_tensor(out=x_, in0=p_, scalar=2.0, in1=x_, op0=ALU.mult, op1=ALU.add))
            dve.wait_ge(dt_parts, 2)
            nc.vector.tensor_scalar(e_, x_, eps_col[0:32, 1:2], -1.0, ALU.mult, ALU.mult).then_inc(dt_ready, 1)
            dve.wait_ge(q_row_stored, 16)
            dve.wait_ge(out_done, 16 * 19)
            for n in range(4):
                dve.wait_ge(st_done[n], 16 * [8, 6, 6, 6][n])
            dve.wait_ge(dt_rows, 1)
            nc.vector.tensor_copy(dt_t[:, :, 0:4], mp[:, 0, 0:320].rearrange("p (k c h) -> p k c h", k=2, c=5)[:, :, 0:4])
            st.link(nc.vector.tensor_copy(dt_t[0:NS, :, 4], mp[0:NS, 0, 0:320].rearrange("p (k c h) -> p k c h", k=2, c=5)[:, :, 4]))
            for b in range(NB):
                z = nc.vector.tensor_scalar(dta_m[:, b], dt_t[0:NS, 1, 4], c_at["bmask"][:, b:b + 1], None, ALU.mult)
            z.then_inc(dt_ready, 1)
            dve.wait_ge(dt_rows, 2)
            dve.wait_ge(dt_parts, 3)
            nc.vector.tensor_copy(a_col[:, 0:4], mp[:, 1, 0:128].rearrange("p (c h) -> p c h", c=4))
            nc.vector.tensor_copy(a_col[0:NS, 4], mp[0:NS, 1, 128:160])
            nc.vector.tensor_copy(a_row[:, 0:SEQ], mp[0:32, 2, :])
            nc.vector.tensor_copy(a_row[:, SEQ:R], mp[0:32, 3, 0:NS]).then_inc(a_row_done, 1)
            dve.wait_ge(a_row_done, 1)
            nc.vector.tensor_tensor(dte[:, 0:4], mp[:, 1, 160:288].rearrange("p (c h) -> p c h", c=4), a_col[:, 0:4], ALU.subtract)
            nc.vector.tensor_tensor(dte[0:NS, 4], mp[0:NS, 1, 288:320], a_col[0:NS, 4], ALU.subtract).then_inc(dt_neg, 1)
            dve.wait_ge(dt_parts, 4)
            nc.vector.tensor_tensor(dte[:, 0:4], dte[:, 0:4], dt_t[:, 0, 0:4], ALU.mult)
            st.link(nc.vector.tensor_tensor(dte[0:NS, 4], dte[0:NS, 4], dt_t[0:NS, 0, 4], ALU.mult))

            def ssd(g, last):
                for c in range(5):
                    sl, w = c % 2, (P if c < 4 else NS)
                    prev = g * 5 + (0 if c == 0 else c - 1)
                    T = g * 5 + (c + 1)
                    hd = bass.ds(g * 8, 8)

                    def cols(t, part):
                        return t.rearrange("p (h o) -> p h o", o=1).to_broadcast([part, 8, HP])
                    dve.wait_ge(bc_in[sl], g * (48 if sl == 0 else 32) + 16 * (c // 2 + 1))
                    wait(dve, y_mm, prev)
                    neg = c_at["neg"] if c < 4 else c_at["neg_s"]
                    for h in range(8):
                        z = nc.vector.scalar_tensor_tensor(
                            out=decay[0:w, sl, h, 0:w], in0=hd_bc[0:w, sl, h, 0:w],
                            scalar=a_col[0:w, c, bass.ds(g * 8 + h, 1)], in1=neg, op0=ALU.subtract, op1=ALU.add)
                    z.then_inc(diff_done, 1)
                    dve.wait_ge(xr_mm, T)
                    wait(dve, st_mm, g * 12 + (0 if c == 0 else c - 1))
                    xr = mp[0:w, 1, :].rearrange("p (h e) -> p h e", h=8)
                    nc.vector.tensor_tensor(x_dt[0:w, sl], xr, cols(dt_t[0:w, 0, c, hd], w), ALU.mult)
                    nc.vector.tensor_tensor(x_end[0:w, sl], xr, cols(dte[0:w, c, hd], w), ALU.mult).then_inc(x_dt_done, 1)
                    dve.wait_ge(ea_done, T)
                    dve.wait_ge(ssd_in, T)
                    nc.vector.tensor_tensor(
                        c_exp[:, sl, :, 0:w], c_exp[:, sl, :, 0:w],
                        ssd_bc[:, sl, 1:2, 0:w].to_broadcast([P, 8, w]), ALU.mult).then_inc(c_exp_done, 1)
                    dve.wait_ge(decay_done, T)
                    dve.wait_ge(b_row_done, T)
                    nc.vector.tensor_tensor(
                        decay[0:w, sl, :, 0:w], decay[0:w, sl, :, 0:w],
                        mp[0:w, 0:1, 0:w].to_broadcast([w, 8, w]), ALU.mult).then_inc(m_done, 1)
                    if c == 4:
                        wait(dve, st_mm, g * 12)
                        for b in range(NB):
                            z = nc.vector.tensor_scalar(b_msk[:, b], b_row[0:NS, sl], c_at["bmask"][:, b:b + 1], None, ALU.mult)
                        z.then_inc(b_msk_done, 1)
                    dve.wait_ge(y_mm, T)
                    for j in range(4):
                        z = nc.vector.scalar_tensor_tensor(
                            out=xbc[:, bass.ds(g * 4 + j, 1), c * P:c * P + w].rearrange("p o n -> p (o n)"),
                            in0=ssd_x[:, sl, j, 0:w], scalar=c_at["d_skip"][:, bass.ds(g * 4 + j, 1)],
                            in1=gp[:, sl, 0, j * P:j * P + w], op0=ALU.mult, op1=ALU.add)
                    z.then_inc(y_done, 1)
                    if c < 4:
                        dve.wait_ge(st_mm, g * 12 + (c + 1))
                        inc = gp[:, c % 2, 1, :].rearrange("p (h e) -> p h e", h=8)
                        if c == 0:
                            wait(dve, h_out, g * 16)
                            nc.vector.tensor_copy(h_t[:], inc).then_inc(state_done, 1)
                        else:
                            dve.wait_ge(state_done, g * 12 + c)
                            st.link(nc.vector.tensor_tensor(h_t[:], h_t[:], cols(ea[:, c, hd], P), ALU.mult))
                            nc.vector.tensor_tensor(h_t[:], h_t[:], inc, ALU.add).then_inc(state_done, 1)
                    else:
                        dve.wait_ge(hs_in, g * 16 + 16)
                        for b in range(NB):
                            st.link(nc.vector.tensor_tensor(hs_t[:, b], hs_t[:, b], cols(eas[:, b, hd], P), ALU.mult))
                            dve.wait_ge(st_mm, g * 12 + (5 + b))
                            nc.vector.tensor_tensor(hs_t[:, b], hs_t[:, b], gp[:, b % 2, 1, :].rearrange("p (h e) -> p h e", h=8),
                                                    ALU.add).then_inc(state_done, 1)
            turns(dve, NG_SSM, ssd, [(st, 11)], peel_first=True)

            def scores_out(call, c2, cc, half):
                I = 16 * call + 2 * cc + half
                g = call % 4
                dve.wait_ge(s_mm, c2 * 4 + (I + 1))
                wait(dve, pt_mm, c2 * 4 + (I - 1))
                if half == 0:
                    wait(dve, o_mm, c2 * 2 + (8 * call + cc - 1))
                slope = at_at["slope"][:, bass.ds(c2 * 4 + (16 * call + 2 * cc + half), 1)]
                wide = call in (0, 1)
                if wide:
                    st.link(nc.vector.scalar_tensor_tensor(
                        out=at_e[:, half, 1:8].rearrange("p a b -> p (a b)"), in0=at_at["dist0"], scalar=slope,
                        in1=gp[:, half].rearrange("p a b -> p (a b)")[:, P:1024], op0=ALU.mult, op1=ALU.add))
                    e = at_e[:, half].rearrange("p (t a) b -> p t (a b)", a=2)
                else:
                    d = at_at["dist1" if call == 2 else "dist2"].rearrange("p (o k) -> p o k", o=1).to_broadcast([P, 4, P])
                    e = at_e[:, half, 0:4]
                    st.link(nc.vector.scalar_tensor_tensor(
                        out=e, in0=d, scalar=slope, in1=gp[:, half, 0, :].rearrange("p (t k) -> p t k", t=4),
                        op0=ALU.mult, op1=ALU.add))
                nc.vector.tensor_reduce(at_st[:, cc, half * 8:half * 8 + 4], e, AX.X, ALU.max,
                                        negate=True).then_inc(nm_done, 1)

            def pt_out(call, c2, cc, half):
                I = 16 * call + 2 * cc + half
                dve.wait_ge(pt_mm, c2 * 4 + (I + 1))
                wait(dve, o_mm, c2 * 2 + (8 * call + cc - 1))
                n = 896 if call in (0, 1) else 512
                nc.vector.tensor_copy(at_pt[:, half].rearrange("p a b -> p (a b)")[:, 0:n],
                                      mp[:, 0:2].rearrange("p a b -> p (a b)")[:, 0:n]).then_inc(pt_done, 1)

            def attention(call):
                if call in (0, 1):
                    nc.vector.memset(at_e[:, 0, 0], NEG)
                    st.link(nc.vector.memset(at_e[:, 1, 0], NEG))
                scores_out(call, 0, 0, 0)

                def body(c2, last):
                    for i in range(4):
                        cc, half = i // 2, i % 2
                        if not (last and i == 3):
                            j = i + 1
                            scores_out(call, c2 + j // 4, (j % 4) // 2, j % 2)
                        pt_out(call, c2, cc, half)
                turns(dve, 3, body, [(st, 4)], peel_first=(call == 0))
                body(3, True)
            dve.wait_ge(atc_in, 16)
            attention(0)

            def samples(lay):
                hb0 = 0 if lay == 0 else 4

                def body(i, last):
                    for sl in range(2):
                        hb = hb0 + sl
                        kind = "sdist0"
                        dve.wait_ge(sms_mm, i * 2 + (hb + 1))
                        wait(dve, smt_mm, i * 2 + (hb - 1))
                        wait(dve, sm_stored[sl], i * 32 + (0 if lay == 0 else 64))
                        st.link(nc.vector.scalar_tensor_tensor(
                            out=sm_e[:, sl], in0=DIST(lay, i), scalar=at_at["sslope"][:, bass.ds(i * 2 + hb, 1)],
                            in1=mp[:, 2 + sl, 0:160], op0=ALU.mult, op1=ALU.add))
                        nc.vector.tensor_reduce(sm_ms[:, sl, 0:1], sm_e[:, sl], AX.X, ALU.max,
                                                negate=True).then_inc(smn_done, 1)
                if lay == 0:
                    turns(dve, 2, body, [(st, 2)], peel_first=True)
                else:
                    for i in range(6):
                        body(i, False)
            samples(0)
            dve.wait_ge(so_mm, 1)
            for kv in range(2):
                for half in range(2):
                    hp = slice(half * HEAD_DIM, (half + 1) * HEAD_DIM)
                    src = mp[kv * HEAD_DIM:(kv + 1) * HEAD_DIM, 0, :].rearrange("p (c h n) -> p c h n", h=2, n=NS)
                    z = nc.vector.tensor_copy(xbc[hp, 16 + 4 * kv:20 + 4 * kv, SEQ:R], src[:, 4 * kv:4 * kv + 4, half])
            z.then_inc(so_done, 1)

            dve.wait_ge(stt_in, 48)
            st.link(nc.vector.tensor_scalar(eps_col[0:16, 2:3], c_at["sink"], -1.0, None, ALU.mult))
            nc.vector.tensor_scalar(fac[:, 1], stt[:, 0, 0], eps_col[0:16, 2:3], None, ALU.min).then_inc(dves2, 1)
            dve.wait_ge(dves2, 1)
            nc.vector.tensor_tensor(fac[:, 0], fac[:, 1], stt[:, 0, 0], ALU.subtract).then_inc(dves2, 1)
            dve.wait_ge(fac_act, 1)
            st.link(nc.vector.tensor_tensor(stt[:, 0, 1], stt[:, 0, 1], fac[:, 0], ALU.mult))
            st.link(nc.vector.tensor_tensor(stt[:, 0, 1], stt[:, 0, 1], fac[:, 2], ALU.add))
            st.link(nc.vector.reciprocal(stt[:, 0, 1], stt[:, 0, 1]))
            nc.vector.tensor_tensor(fac[:, 0], fac[:, 0], stt[:, 0, 1], ALU.mult).then_inc(fac_done, 1)

            def merge(lay):
                per = 32 if lay == 0 else 96
                def body(i, last):
                    for sl in range(2):
                        C = bass.ds(i * 2 + sl, 1)
                        dve.wait_ge(f_in[sl], i * per + ((0 if lay == 0 else 128) + per))
                        wait(dve, b_hi_done, i * 2 + (BB[f"attn{lay}"] + sl - 1))
                        if lay == 0:
                            nc.vector.tensor_tensor(xw[:, sl:sl + 1], xbc[:, bass.ds(i * 2 + (16 + sl), 1)],
                                                    f_bc[:, sl, 0:1], ALU.mult).then_inc(merged, 1)
                        else:
                            st.link(nc.vector.tensor_tensor(xw[:, sl:sl + 1], o_t[0][:, C], f_bc[:, sl, 0:1], ALU.mult))
                            for g in (1, 2):
                                d = DIL[g]
                                nc.vector.tensor_tensor(
                                    sq[:, sl, 0:SEQ].rearrange("p (n r) -> p n r", r=d),
                                    o_t[g][:, C, 0:SEQ].rearrange("p o (r n) -> p n (o r)", r=d),
                                    f_bc[:, sl, g, 0:SEQ].rearrange("p (n r) -> p n r", r=d), ALU.mult)
                                st.link(nc.vector.tensor_tensor(sq[:, sl:sl + 1, SEQ:R], o_t[g][:, C, SEQ:R],
                                                                f_bc[:, sl, g:g + 1, SEQ:R], ALU.mult))
                                z = nc.vector.tensor_tensor(xw[:, sl], xw[:, sl], sq[:, sl], ALU.add)
                                if g == 1:
                                    st.link(z)
                                else:
                                    z.then_inc(merged, 1)
                        dve.wait_ge(b_hi_done, i * 2 + (BB[f"attn{lay}"] + sl + 1))
                        nc.vector.tensor_tensor(b_lo[:, C], xw[:, sl:sl + 1], b_hi[:, C].bitcast(F32),
                                                ALU.subtract).then_inc(b_ready, 1)
                turns(dve, 4, body, [(st, 8)] if lay else (), peel_first=(lay == 0))
            merge(0)

            def split_n(G):
                if G >= G_END:
                    return
                dve.wait_ge(w_hi_done, G + 1)
                nc.vector.tensor_tensor(w_lo[:, G % 2], w_raw[:, G % 2], w_hi[:, G % 2].bitcast(F32),
                                        ALU.subtract).then_inc(w_lo_done, 1)

            def add_x(ph, it, n):
                xc = x_t[:, bass.ds(it * 4 + n, 1)].rearrange("p o (h n) -> p (o h) n", h=2)
                nc.vector.tensor_tensor(xc, xc, gp[:, n % 2, :, 0:HALF], ALU.add).then_inc(drained, 1)

            for g in range(4):
                G = G0["out0_0"] + g
                split_n(G + 1)
                for j in range(4):
                    C = 4 * g + j
                    dve.wait_ge(z_silu, C + 1)
                    nc.vector.tensor_tensor(xbc[:, C], xbc[:, C], xbc[:, 16 + C % 8], ALU.mult).then_inc(gated, 1)
                for c in range(2):
                    dve.wait_ge(mm_done, 2 * G + c + 1)
                    add_x("out0_0", 0, 2 * g + c)
                dve.wait_ge(gate_rms, g + 1)
                st.link(nc.vector.reciprocal(rstd8[:], rstd8[:]))
                for j in range(4):
                    C = 4 * g + j
                    nc.vector.scalar_tensor_tensor(out=xbc[:, C], in0=xbc[:, C], scalar=c_at["ssm_norm"][:, C:C + 1],
                                                   in1=rstd8[:], op0=ALU.mult, op1=ALU.mult).then_inc(y_ready, 1)
                if g < 2:
                    for j in range(4):
                        C = 4 * g + j
                        dve.wait_ge(a_hi_done, AB["y"] + C + 1)
                        nc.vector.tensor_tensor(a_lo[:, C], xbc[:, C], a_hi[:, C].bitcast(F32),
                                                ALU.subtract).then_inc(a_ready, 1)

            def body(it, last):
                for s in range(2):
                    split("out0_1", it, s)
                    for c in range(2):
                        n = 2 * s + c
                        dve.wait_ge(b_hi_done, it * 4 + (BB["y"] + n + 1))
                        nc.vector.tensor_tensor(b_lo[:, bass.ds(it * 4 + n, 1)], xbc[:, bass.ds(it * 4 + (8 + n), 1)],
                                                b_hi[:, bass.ds(it * 4 + n, 1)].bitcast(F32), ALU.subtract).then_inc(b_ready, 1)
                        dve.wait_ge(mm_done, it * 4 + (2 * G0["out0_1"] + n + 1))
                        add_x("out0_1", it, n)
            turns(dve, 2, body)

            def final_parts(i, it, n, drained_at, it_per=4, chunk=None):
                C = bass.ds(it * 4 + n, 1)
                flat = lambda t: t.rearrange("p o n -> p (o n)")
                if i < 4:
                    dve.wait_ge(drained, drained_at)
                    dve.wait_ge(a_hi_done, it * 4 + (AB[i] + n - 1))
                    nc.vector.tensor_scalar(xw[:, n % 2], flat(x_t[:, C]),
                                            norm_w[:, i:i + 1, bass.ds(it * 4 + n, 1)].rearrange("p a b -> p (a b)"), None,
                                            ALU.mult).then_inc(a_w, 1)
                    dve.wait_ge(a_hi_done, it * 4 + (AB[i] + n + 1))
                    nc.vector.tensor_tensor(flat(a_lo[:, C]), xw[:, n % 2], flat(a_hi[:, C]).bitcast(F32),
                                            ALU.subtract).then_inc(a_ready, 1)
                dve.wait_ge(sq_done, it * 4 + (8 * i + n + 1))
                if n > 0 or not isinstance(it, int):
                    dve.wait_ge(ssq_done, it * 4 + (8 * i + n))
                if n == 0 and isinstance(it, int) and it == 0:
                    nc.vector.tensor_copy(ssq[:], sq[:, 0]).then_inc(ssq_done, 1)
                else:
                    nc.vector.tensor_tensor(ssq[:], ssq[:], sq[:, n % 2], ALU.add).then_inc(ssq_done, 1)

            def body(it, last):
                for s in range(2):
                    split("out0_2", it, s)
                    for c in range(2):
                        n = 2 * s + c
                        at_n = it * 4 + (2 * G0["out0_2"] + n + 1)
                        dve.wait_ge(mm_done, at_n)
                        add_x("out0_2", it, n)
                        final_parts(1, it, n, at_n)
            turns(dve, 2, body, peel_first=True)
            inverse_rms(1)

            def mlp(lay, i_norm):
                ph = f"mlp{lay}"

                def one(j, G):
                    G += G0[ph]
                    if isinstance(j, int) and 8 * j + G + 1 >= G_END:
                        return
                    s1 = (G + 1) % 2
                    dve.wait_ge(w_hi_done, j * 8 + (G + 2))
                    nc.vector.tensor_tensor(w_lo[:, s1], w_raw[:, s1], w_hi[:, s1].bitcast(F32),
                                            ALU.subtract).then_inc(w_lo_done, 1)

                def body(j, last):
                    for i in range(4):
                        one(j, i)
                        for c in range(2):
                            n = 2 * i + c
                            at_n = j * 16 + (2 * G0[ph] + n + 1)
                            dve.wait_ge(mm_done, at_n)
                            dve.wait_ge(b_hi_done, j * 8 + (BB[ph] + n - 1))
                            nc.vector.tensor_tensor(xw[:, c].rearrange("p (h n) -> p h n", h=2), gp[:, c, :, 0:HALF],
                                                    rstd[:].rearrange("p (h n) -> p h n", h=2), ALU.mult).then_inc(drained, 1)
                            dve.wait_ge(drained, at_n)
                            nc.vector.scalar_tensor_tensor(out=xw[:, c], in0=xw[:, c], scalar=0.0, in1=xw[:, c],
                                                           op0=ALU.max, op1=ALU.mult).then_inc(h_val, 1)
                            dve.wait_ge(b_hi_done, j * 8 + (BB[ph] + n + 1))
                            dve.wait_ge(h_val, j * 8 + (32 * lay + n + 1))
                            nc.vector.tensor_tensor(b_lo[:, n], xw[:, c], b_hi[:, n].bitcast(F32),
                                                    ALU.subtract).then_inc(b_ready, 1)
                    for i in range(4):
                        one(j, 4 + i)
                        for c in range(2):
                            n = 2 * i + c
                            at_n = j * 16 + (2 * G0[ph] + 8 + n + 1)
                            dve.wait_ge(mm_done, at_n)
                            add_x(ph, 0, n)
                            if last:
                                final_parts(i_norm, 0, n, at_n)
                turns(dve, 4, body, peel_last=True)
            mlp(0, 2)
            inverse_rms(2)

            def odd(kind, g):
                ph = f"odd_{kind}{g}"
                W, d = odd_at(ph), DIL[g]
                scale = rstd8 if kind == "q" else rstd

                def body(it, last):
                    for s in range(2):
                        split(ph, it, s)
                        for c in range(2):
                            n = 2 * s + c
                            dve.wait_ge(mm_done, it * 4 + (2 * G0[ph] + n + 1))
                            if kind == "v":
                                wait(dve, st1[n], 16 * 12)
                            else:
                                wait(dve, st1[n], it * 16 + 8 * W)
                            wait(dve, rows1_mm, it * 2 + (W + s - 1))
                            if d == 1:
                                nc.vector.tensor_tensor(stage1[:, n].rearrange("p (h n) -> p h n", h=2), gp[:, c, :, 0:HALF],
                                                        scale[:].rearrange("p (h n) -> p h n", h=2),
                                                        ALU.mult).then_inc(drained, 1)
                                continue
                            dst = stage1[:, n, 0:SEQ].rearrange("p (r n) -> p n r", r=d)
                            nc.vector.tensor_tensor(dst[:, 0:HALF // d], gp[:, c, 0, 0:HALF].rearrange("p (n r) -> p n r", r=d),
                                                    scale[:, 0:HALF].rearrange("p (n r) -> p n r", r=d), ALU.mult)
                            nc.vector.tensor_tensor(dst[:, HALF // d:SEQ // d],
                                                    gp[:, c, 1, 0:SEQ - HALF].rearrange("p (n r) -> p n r", r=d),
                                                    scale[:, HALF:SEQ].rearrange("p (n r) -> p n r", r=d), ALU.mult)
                            nc.vector.tensor_tensor(stage1[:, n, SEQ:R], gp[:, c, 1, SEQ - HALF:HALF], scale[:, SEQ:R],
                                                    ALU.mult).then_inc(drained, 1)
                        if kind == "q":
                            continue
                        U = W - 12 + s
                        b = it * 2 + (s + (0 if kind == "k" else 4))
                        dve.wait_ge(u1_in[s], it * 32 + 16 * (W - 12) + 32)
                        k = u1_k[:, s] if g else u1_k[:, s, 0:1].to_broadcast([P, NT, D])
                        st.link(nc.vector.tensor_tensor(u1_q[s][:], u1_q[s][:], k, ALU.mult))
                        nc.vector.tensor_reduce(s1_t[:, 16 * g:16 * g + 16, bass.ds(b * NT, NT)].rearrange("p h t -> p t h"),
                                                u1_q[s][:].rearrange("p t (h e) -> p t h e", e=HEAD_DIM), AX.X,
                                                ALU.add).then_inc(unit1_done, 1)
                turns(dve, 2, body, [(st, 2)] if kind != "q" else (), peel_first=(ph == "odd_q0"))
            for kind, g in ODD:
                odd(kind, g)

            projection_stored(dve)
            dve.wait_ge(atc_in, 32)
            for call in (1, 2, 3):
                attention(call)
            samples(1)
            for g in range(3):
                dve.wait_ge(v_used, (8, 40, 72)[g])
                for half in range(2):
                    hp = slice(half * HEAD_DIM, (half + 1) * HEAD_DIM)
                    st.link(nc.vector.tensor_copy(o_t[g][hp, :, SEQ:R],
                                                  mp[hp, g, :].rearrange("p (c h n) -> p c h n", h=2, n=NS)[:, :, half]))

            dve.wait_ge(stt_in, 192)
            for g, d in enumerate(DIL):
                st.link(nc.vector.tensor_copy(nat[:, g, :, 0:SEQ].rearrange("p k (n r) -> p k n r", r=d),
                                              stt[:, g, :, 0:SEQ].rearrange("p k (r n) -> p k n r", r=d)))
                st.link(nc.vector.tensor_copy(nat[:, g, :, SEQ:R], stt[:, g, :, SEQ:R]))
            low = stt[:, 0, 0]
            st.link(nc.vector.tensor_tensor(low, nat[:, 0, 0], nat[:, 1, 0], ALU.min))
            st.link(nc.vector.tensor_tensor(low, low, nat[:, 2, 0], ALU.min))
            nc.vector.tensor_tensor(fac[:], stt[:, 0, 0:1].to_broadcast([16, 3, R]), nat[:, :, 0], ALU.subtract).then_inc(dves2, 1)
            dve.wait_ge(fac_act, 2)
            st.link(nc.vector.tensor_tensor(nat[:, :, 1], nat[:, :, 1], fac[:], ALU.mult))
            st.link(nc.vector.tensor_tensor(low, nat[:, 0, 1], nat[:, 1, 1], ALU.add))
            st.link(nc.vector.tensor_tensor(low, low, nat[:, 2, 1], ALU.add))
            st.link(nc.vector.reciprocal(low, low))
            nc.vector.tensor_tensor(fac[:], fac[:], stt[:, 0, 0:1].to_broadcast([16, 3, R]), ALU.mult).then_inc(fac_done, 1)
            merge(1)

            def body(it, last):
                for s in range(2):
                    split("out1", it, s)
                    for c in range(2):
                        n = 2 * s + c
                        at_n = it * 4 + (2 * G0["out1"] + n + 1)
                        dve.wait_ge(mm_done, at_n)
                        add_x("out1", it, n)
                        final_parts(3, it, n, at_n)
            turns(dve, 2, body, peel_first=True)
            inverse_rms(3)
            mlp(1, 4)
            inverse_rms(4)
            for c in range(KC):
                nc.vector.scalar_tensor_tensor(out=x_t[:, c], in0=x_t[:, c], scalar=norm_w[:, 4, c:c + 1], in1=rstd[:],
                                               op0=ALU.mult, op1=ALU.mult).then_inc(y_out, 1)

        @block.tensor
        def _(pe):
            def stats(i):
                pe.wait_ge(ssq_done, KC * (i + 1))
                if i == 0:
                    pe.wait_ge(ones_set, 1)
                for h in range(2):
                    m = nc.tensor.matmul(mp[:, h, 0:HALF], ones[:], ssq[:, h * HALF:(h + 1) * HALF],
                                         start=True, stop=True)
                m.then_inc(stat_mm, 1)

            def group(ph, it, s, hi, lo, ready, ready_at, chunks=(0, 1), sl=None, turn=2, ready_per=0):
                G = G0[ph] + s
                sl = s if sl is None else sl
                pe.wait_ge(w_lo_done, it * turn + (G + 1))
                for c in range(2):
                    wait(pe, drained, it * (2 * turn) + (2 * G + c - 1))
                    if c not in chunks:
                        nc.tensor.nop().then_inc(mm_done, 1)
                        continue
                    n = 0
                    for k in range(KC):
                        if c == 0:
                            pe.wait_ge(ready, it * ready_per + (ready_at + k + 1) if ready_per else ready_at + k + 1)
                        for w, x in ((w_hi, hi), (w_lo, hi), (w_hi, lo)):
                            for h in range(2):
                                m = nc.tensor.matmul(gp[:, c, h, 0:HALF], w[:, sl, k, c * P:(c + 1) * P],
                                                     x[:, k, h * HALF:(h + 1) * HALF], start=n < 2, stop=n >= 46)
                                n += 1
                    m.then_inc(mm_done, 1)
            stats(0)

            def body(it, last):
                for s in range(2):
                    group("xbc", it, s, a_hi, a_lo, a_ready, 0)
            turns(pe, NG["xbc"] // 2, body, peel_first=True)

            E_ = G0["kv_dt"]
            group("kv_dt", 0, 0, a_hi, a_lo, a_ready, 0)
            pe.wait_ge(drained, 2 * E_ + 2)
            pe.wait_ge(consts_in, 80)
            for t in range(4):
                nc.tensor.transpose(mp[:, 2, t * P:(t + 1) * P], stage[:, 1, t * P:(t + 1) * P], ident[:])
            nc.tensor.transpose(mp[0:NS, 3, 0:P], stage[:, 0, SEQ:R], ident[:])
            nc.tensor.transpose(mp[0:NS, 3, P:2 * P], stage[:, 1, SEQ:R], ident[:]).then_inc(v_turned, 1)
            group("kv_dt", 0, 1, a_hi, a_lo, a_ready, 0, chunks=(1,))

            def body(it, last):
                for s in range(2):
                    group("q", it, s, a_hi, a_lo, a_ready, 0)
                    pe.wait_ge(drained, it * 4 + (2 * G0["q"] + 2 * s + 2))
                    wait(pe, rows_out, it * 2 + (s + 2))
                    for c in range(2):
                        m = nc.tensor.transpose(mp[0:NS, 3, c * P:(c + 1) * P], stage[:, 2 * s + c, SEQ:R], ident[:])
                    m.then_inc(q_turned, 1)
            turns(pe, NG["q"] // 2, body)

            def body(it, last):
                for s in range(2):
                    group("z", it, s, a_hi, a_lo, a_ready, 0)
            turns(pe, NG["z"] // 2, body)

            pe.wait_ge(dt_ready, 1)
            pe.wait_ge(rows_out, 2 + NG["q"])
            for k, src in ((0, dt_w[:, 0]), (1, dt_w[:, 1])):
                for c in range(5):
                    w = P if c < 4 else NS
                    m = nc.tensor.transpose(mp[0:w, 0, k * 160 + c * 32:k * 160 + c * 32 + 32], src[:, c * P:c * P + w], ident[0:32, 0:32])
            m.then_inc(dt_rows, 1)
            pe.wait_ge(dt_ready, 2)
            for c in range(5):
                w = P if c < 4 else NS
                tri, one = (c_at["tri"], ones[:]) if c < 4 else (c_at["tri_s"], c_at["ones_s"])
                rhs = dt_t[0:w, 1, c]
                nc.tensor.matmul(mp[0:w, 1, c * 32:c * 32 + 32], tri, rhs, start=True, stop=True)
                nc.tensor.matmul(mp[0:w, 1, 160 + c * 32:160 + c * 32 + 32], one, rhs, start=True, stop=True)
                dst = mp[0:32, 2, c * P:c * P + P] if c < 4 else mp[0:32, 3, 0:NS]
                nc.tensor.matmul(dst, rhs, tri, start=True, stop=True)
            m = nc.tensor.matmul(mp[:, 3, 32:288], ones[0:NS, :], dta_m[:].rearrange("p b h -> p (b h)"), start=True, stop=True)
            m.then_inc(dt_rows, 1)
            pe.wait_ge(dt_neg, 2)
            pe.wait_ge(dt_parts, 3)

            def ssd(g, last):
                for c in range(5):
                    sl, w = c % 2, (P if c < 4 else NS)
                    prev = g * 5 + (0 if c == 0 else c - 1)
                    T = g * 5 + (c + 1)
                    pe.wait_ge(ssd_in, T)
                    wait(pe, m_done, g * 5 + c)
                    wait(pe, x_dt_done, g * 5 + c)
                    nc.tensor.matmul(mp[0:w, 0, 0:w], ssd_bc[:, sl, 0, 0:w], ssd_bc[:, sl, 1, 0:w], start=True, stop=True)
                    nc.tensor.transpose(mp[0:w, 0, P:2 * P], ssd_bc[:, sl, 0, 0:w], ident[:]).then_inc(cb_mm, 1)
                    for j in range(4):
                        m = nc.tensor.transpose(mp[0:w, 1, j * P:(j + 1) * P], ssd_x[:, sl, j, 0:w], ident[:])
                    m.then_inc(xr_mm, 1)
                    pe.wait_ge(m_done, T)
                    pe.wait_ge(c_exp_done, T)
                    wait(pe, y_done, prev)
                    if c == 4:
                        pe.wait_ge(hs_in, g * 16 + 16)
                    elif c > 0:
                        pe.wait_ge(state_done, g * 12 + c)
                    for h in range(8):
                        half, j = h % 2, h // 2
                        ph = slice(half * HP, half * HP + HP)
                        m = nc.tensor.matmul(gp[ph, sl, 0, j * P:j * P + w], x_dt[0:w, sl, h], decay[0:w, sl, h, 0:w],
                                             start=True, stop=(c == 0), skip_group_check=True)
                        if 0 < c < 4:
                            m = nc.tensor.matmul(gp[ph, sl, 0, j * P:j * P + w], h_t[:, h], c_exp[:, sl, h, 0:w],
                                                 start=False, stop=True, skip_group_check=True)
                        for b in range(NB if c == 4 else 0):
                            m = nc.tensor.matmul(gp[ph, sl, 0, j * P + b * NT:j * P + (b + 1) * NT], hs_t[:, b, h],
                                                 c_exp[:, sl, h, b * NT:(b + 1) * NT], start=False, stop=True,
                                                 skip_group_check=True)
                    m.then_inc(y_mm, 1)
                    if c < 4:
                        pe.wait_ge(b_row_done, T)
                        wait(pe, state_done, g * 12 + (c - 1))
                        nc.tensor.matmul(gp[:, c % 2, 1, :], b_row[0:w, sl], x_end[0:w, sl].rearrange("p h e -> p (h e)"),
                                         start=True, stop=True).then_inc(st_mm, 1)
                    else:
                        pe.wait_ge(b_msk_done, g + 1)
                        for b in range(NB):
                            pe.wait_ge(state_done, g * 12 + (3 + b))
                            nc.tensor.matmul(gp[:, b % 2, 1, :], b_msk[:, b], x_end[0:NS, sl].rearrange("p h e -> p (h e)"),
                                             start=True, stop=True).then_inc(st_mm, 1)
            turns(pe, NG_SSM, ssd, peel_first=True)

            def scores(call, c2, cc, half):
                I = 16 * call + 2 * cc + half
                per = 80 if call == 0 else 48
                base = 0 if call == 0 else 320 + (call - 1) * 192
                pe.wait_ge(at_in[cc], c2 * per + (base + per))
                wait(pe, nm_done, c2 * 4 + (I - 1))
                hp = slice(half * HEAD_DIM, (half + 1) * HEAD_DIM)
                for t in range(4):
                    if call in (0, 1):
                        k0 = max(t - 1, 0) * P
                        dst = gp[:, half, t // 2, (t % 2) * 256 + (P if t == 0 else 0):(t % 2) * 256 + 256]
                        k = at_k[hp, cc, k0:(t + 1) * P]
                    else:
                        dst = gp[:, half, 0, t * P:(t + 1) * P]
                        k = at_k[hp, cc, t * P:(t + 1) * P]
                    m = nc.tensor.matmul(dst, at_q[hp, cc, t * P:(t + 1) * P], k, start=True, stop=True)
                m.then_inc(s_mm, 1)

            def turn_exp(call, c2, cc, half):
                I = 16 * call + 2 * cc + half
                pe.wait_ge(p_done, c2 * 4 + (I + 1))
                wait(pe, pt_done, c2 * 4 + I)
                n = 7 if call in (0, 1) else 4
                flat = mp[:, 0:2].rearrange("p a b -> p (a b)")
                for j in range(n):
                    e = at_e[:, half, j + (n == 7)]
                    m = nc.tensor.transpose(flat[:, j * P:(j + 1) * P], e, ident[:])
                m.then_inc(pt_mm, 1)

            def times_v(call, c2, cc, half):
                I = 16 * call + 2 * cc + half
                pe.wait_ge(pt_done, c2 * 4 + (I + 1))
                if half == 0:
                    wait(pe, o_done, c2 * 2 + (8 * call + cc))
                hp = slice(half * HEAD_DIM, (half + 1) * HEAD_DIM)
                for t in range(4):
                    out = mp[hp, 2, t * P:(t + 1) * P]
                    if call in (0, 1) and t > 0:
                        nc.tensor.matmul(out, at_v[:, cc, t - 1, hp], at_pt[:, half, 2 * t - 1], start=True, stop=False)
                        m = nc.tensor.matmul(out, at_v[:, cc, t, hp], at_pt[:, half, 2 * t], start=False, stop=True)
                    else:
                        m = nc.tensor.matmul(out, at_v[:, cc, t, hp], at_pt[:, half, t], start=True, stop=True)
                if half == 1:
                    nc.tensor.transpose(mp[0:16, 3, 0:P], at_st[:, cc], ident[:]).then_inc(o_mm, 1)

            def attention(call):
                scores(call, 0, 0, 0)

                def body(c2, last):
                    for i in range(4):
                        if not (last and i == 3):
                            j = i + 1
                            scores(call, c2 + j // 4, (j % 4) // 2, j % 2)
                        turn_exp(call, c2, i // 2, i % 2)
                        j = i - 1
                        if j >= 0:
                            times_v(call, c2, j // 2, j % 2)
                        elif not (isinstance(c2, int) and c2 == 0):
                            times_v(call, c2 - 1, 1, 1)
                turns(pe, 4, body, peel_first=True, peel_last=True)
                times_v(call, 3, 1, 1)
            pe.wait_ge(state_done, 12 * NG_SSM)
            attention(0)

            def samples(lay):
                hb0 = 0 if lay == 0 else 4
                sm_base = 0 if lay == 0 else 96

                def body(i, last):
                    for sl in range(2):
                        hb = hb0 + sl
                        bank = 2 + sl
                        pe.wait_ge(sms_done, i * 2 + (hb + 1))
                        pe.wait_ge(sm_in[sl], i * (48 if lay == 0 else 32) + (sm_base + (48 if lay == 0 else 32)))
                        wait(pe, smt_done, i * 2 + (hb - 1))
                        nc.tensor.transpose(mp[:, bank, 0:P], sm_st[:, sl], ident[:])
                        for h in range(4):
                            hp = slice((h % 2) * HEAD_DIM, (h % 2 + 1) * HEAD_DIM)
                            m = nc.tensor.matmul(mp[h * NS:(h + 1) * NS, bank, P:P + NS], sm_q[hp, sl, h // 2],
                                                 sm_k[hp, sl, 0 if lay == 0 else h // 2], start=True, stop=True)
                        m.then_inc(sms_mm, 1)
                        pe.wait_ge(smp_done, i * 2 + (hb + 1))
                        nc.tensor.transpose(mp[:, bank, 160:288], sm_e[:, sl, 0:P], ident[:])
                        nc.tensor.transpose(mp[0:NS, bank, 288:416], sm_e[:, sl, P:160], ident[:]).then_inc(smt_mm, 1)
                turns(pe, 2 if lay == 0 else 6, body, peel_first=(lay == 0))
            pe.wait_ge(o_done, 8)
            samples(0)
            pe.wait_ge(vn_in, 32)
            pe.wait_ge(smt_done, 4)
            nc.tensor.matmul(mp[:, 0, :], vn[:, 0:P], sm_pn[:, 0:4].rearrange("p a b -> p (a b)"), start=True, stop=False,
                             skip_group_check=True)
            out = mp[:, 0, :].rearrange("p (h n) -> p h n", n=NS)
            pt = sm_pt[:, 0:4].rearrange("p a (h n) -> p (a h) n", n=NS)
            for b in range(NB):
                m = nc.tensor.matmul(out[:, :, b * NT:(b + 1) * NT], v0s[:, b], pt[:, :, b * NT:(b + 1) * NT],
                                     start=False, stop=(b == NB - 1), skip_group_check=True)
            m.then_inc(so_mm, 1)

            for g in range(4):
                group("out0_0", 0, g, b_hi, b_lo, b_ready, BB["attn0"], sl=g % 2)
                for j in range(4):
                    C = 4 * g + j
                    pe.wait_ge(gate_sq, C + 1)
                    if j == 0:
                        wait(pe, gate_rms, g)
                        pe.wait_ge(so_done, 1)
                    for h in range(2):
                        m = nc.tensor.matmul(mp[:, h, 0:HALF], ones[:], sq[:, C % 2, h * HALF:(h + 1) * HALF],
                                             start=(j == 0), stop=(j == 3))
                    m.then_inc(gate_mm, 1)

            def body(it, last):
                for s in range(2):
                    group("out0_1", it, s, a_hi, a_lo, a_ready, AB["y"])
            turns(pe, 2, body)

            def body(it, last):
                for s in range(2):
                    group("out0_2", it, s, b_hi, b_lo, b_ready, BB["y"])
            turns(pe, 2, body)
            stats(1)

            def mlp(lay, i_norm):
                ph = f"mlp{lay}"

                def body(j, last):
                    for i in range(4):
                        group(ph, j, i, a_hi, a_lo, a_ready, AB[i_norm], sl=i % 2, turn=8)
                    for i in range(4):
                        group(ph, j, 4 + i, b_hi, b_lo, b_ready, BB[ph], sl=i % 2, turn=8, ready_per=8)
                turns(pe, 4, body)
            mlp(0, 1)
            stats(2)

            def odd(kind, g):
                ph = f"odd_{kind}{g}"
                W = odd_at(ph)

                def body(it, last):
                    for s in range(2):
                        group(ph, it, s, a_hi, a_lo, a_ready, AB[2])
                        pe.wait_ge(drained, it * 4 + (2 * G0[ph] + 2 * s + 2))
                        if kind == "v":
                            wait(pe, v1_done, it * 2 + (4 * g + s))
                            for c in range(2):
                                for t in range(4):
                                    m = nc.tensor.transpose(mp[:, c, t * P:(t + 1) * P],
                                                            stage1[:, 2 * s + c, t * P:(t + 1) * P], ident[:])
                            m.then_inc(v1_mm, 1)
                        wait(pe, rows1_done, it * 2 + (W + s))
                        for c in range(2):
                            m = nc.tensor.transpose(mp[0:NS, 3, c * P:(c + 1) * P], stage1[:, 2 * s + c, SEQ:R], ident[:])
                        m.then_inc(rows1_mm, 1)
                turns(pe, 2, body, peel_first=(ph in ("odd_q0", "odd_v0")))
            for kind, g in ODD:
                odd(kind, g)
            for call in (1, 2, 3):
                attention(call)
            pe.wait_ge(o_done, 32)
            samples(1)

            pe.wait_ge(vn_in, 48)
            pe.wait_ge(smt_done, 16)
            pt = sm_pt[:].rearrange("p a (h n) -> p a h n", n=NS)
            for g in range(3):
                out = mp[:, g, :].rearrange("p (c h n) -> p c h n", h=2, n=NS)
                for c in range(KC):
                    nc.tensor.matmul(mp[:, g, c * 64:(c + 1) * 64], vn[:, g * D + c * P:g * D + (c + 1) * P],
                                     sm_pn[:, 4 * g + c // 2, (c % 2) * 64:(c % 2) * 64 + 64], start=(c == 0), stop=False,
                                     skip_group_check=True)

                def body(it, last):
                    for j in range(4):
                        pe.wait_ge(v_in[j], it * 16 + 16 * ((0, 2, 10)[g] + 1))
                        col = bass.ds(it * 16 + j * 4, 4) if g == 0 else bass.ds(it * 4 + j, 1)
                        for c in range(KC):
                            m = nc.tensor.matmul(out[:, c, :, col], v1s[:, j, c * P:(c + 1) * P],
                                                 pt[:, 4 * g + c // 2, 2 * (c % 2):2 * (c % 2) + 2, col], start=False,
                                                 stop=True, skip_group_check=True)
                        m.then_inc(v_used, 1)
                turns(pe, 2 if g == 0 else 8, body)

            def body(it, last):
                for s in range(2):
                    group("out1", it, s, b_hi, b_lo, b_ready, BB["attn1"])
            turns(pe, 2, body)
            stats(3)
            mlp(1, 3)
            stats(4)

        @block.gpsimd
        def _(pool):
            E_ = G0["kv_dt"]
            pool.wait_ge(drained, 2 * E_ + 2)
            pool.dma_start(scratch["k0"], stage[:, 0]).then_inc(st_done[0], 16)
            pool.dma_start(o["swa_kp"], stage[:, 0, SEQ - P:SEQ]).then_inc(st_done[0], 16)
            pool.wait_ge(rows_out, 2)
            pool.dma_start(scratch["v0"].rearrange("(t p) f -> p t f", p=P), v_row0[:]).then_inc(out_done, 16)
            pool.dma_start(o["swa_vp"], v_row0[:, 3]).then_inc(out_done, 16)
            for j, nm in ((0, "swa_ks"), (1, "swa_vs")):
                for b in range(NB):
                    pool.dma_start(o[nm][b, P - NT:P], kv_new0[b * NT:(b + 1) * NT, j]).then_inc(out_done, 16)

            def store(ph, dst):
                def body(it, last):
                    for s in range(2):
                        for c in range(2):
                            n = 2 * s + c
                            pool.wait_ge(drained, it * 4 + (2 * G0[ph] + n + 1))
                            pool.dma_start(dst[bass.ds(it * 4 + n, 1)].rearrange("o p n -> p (o n)"),
                                           stage[:, n]).then_inc(st_done[n], 16)
                turns(pool, NG[ph] // 2, body)
            pool.dma_start(scratch["vn0"], kv_new0[:, 1]).then_inc(out_done, 16)
            store("q", scratch["q0"])
            pool.wait_ge(rows_out, 2 + NG["q"])
            pool.dma_start(scratch["q_row0"], q_new0[:]).then_inc(q_row_stored, 16)
            pool.wait_ge(q_row_stored, 16)
            pool.wait_ge(xbc_ready, XC)

            def body(it, last):
                for s in range(2):
                    wait(pool, unit_done, it * 8 + (4 * s - 4))
                    pool.dma_start(u_k[:, s], a["swa_k"][bass.ds(it * 2 + s, 1)].rearrange("o s f -> s (o f)")).then_inc(uk_in[s], 16)
                    for t in range(NT):
                        wait(pool, unit_done, it * 8 + (4 * s + t - 1))
                        pool.dma_start(u_q[:, t % 2].rearrange("p h e -> p (h e)"),
                                       scratch["q_row0"][bass.ds(it * 8 + (4 * s + t), 1)].to_broadcast([P, D])).then_inc(uq_in[t % 2], 16)
                    for c in range(2):
                        n = 2 * s + c
                        pool.wait_ge(drained, it * 4 + (2 * G0["z"] + n + 1))
                        pool.dma_start(scratch["z0"][bass.ds(it * 4 + n, 1)].rearrange("o p n -> p (o n)"),
                                       stage[:, n]).then_inc(st_done[n], 16)
            turns(pool, NG["z"] // 2, body, peel_first=True)
            pool.wait_ge(out_done, 16 * 19)
            pool.wait_ge(out_hw, 16)
            def ssd(g, last):
                for c in range(5):
                    sl, w = c % 2, (P if c < 4 else NS)
                    wait(pool, y_done, g * 5 + (0 if c == 0 else c - 1))
                    nc.gpsimd.tensor_copy(ssd_x[:, sl, :, 0:w], xbc[:, bass.ds(g * 4, 4), c * P:c * P + w])
                    nc.gpsimd.tensor_copy(ssd_bc[:, sl, 0:1, 0:w], xbc[:, bass.ds(g + 16, 1), c * P:c * P + w])
                    nc.gpsimd.tensor_copy(ssd_bc[:, sl, 1:2, 0:w], xbc[:, bass.ds(g + 20, 1), c * P:c * P + w]).then_inc(ssd_in, 1)
                    if c == 4:
                        pool.wait_ge(state_done, g * 12 + 4)
                        pool.dma_start(o["ssm_p"][bass.ds(g, 1)].rearrange("o n f -> n (o f)"),
                                       h_t[:].rearrange("p h e -> p (h e)")).then_inc(h_out, 16)
                        pool.wait_ge(state_done, g * 12 + 12)
                        pool.dma_start(o["ssm_s"][bass.ds(g, 1)].rearrange("o n b f -> n (o b f)"),
                                       hs_t[:].rearrange("p b h e -> p (b h e)")).then_inc(hs_out, 16)
            for n in range(4):
                pool.wait_ge(st_done[n], 16 * [8, 6, 6, 6][n])
            turns(pool, NG_SSM, ssd, peel_first=True)

            def attention_stores(call):
                def body(c2, last):
                    for cc in range(2):
                        C = c2 * 2 + cc
                        dst = scratch["stats"][call][bass.ds(C * 16, 16)]
                        pool.wait_ge(o_done, C + (8 * call + 1))
                        pool.dma_start(dst, at_sr[:, cc]).then_inc(at_stored[cc], 16)
                turns(pool, 4, body)
            attention_stores(0)

            def sample_stores(lay):
                def body(i, last):
                    for sl in range(2):
                        hb0 = 0 if lay == 0 else 4
                        pool.wait_ge(smp_done, i * 2 + (hb0 + sl + 1))
                        for k in range(2):
                            dst = scratch["stats_s"][k].rearrange("h n -> (h n)")[bass.ds(i * 256 + (hb0 + sl) * P, P)]
                            pool.dma_start(dst.rearrange("(p o) -> p o", o=1), sm_ms[:, sl, k:k + 1]).then_inc(sm_stored[sl], 16)
                turns(pool, 2 if lay == 0 else 6, body)
            sample_stores(0)

            pool.wait_ge(b_hi_done, 48)
            pool.wait_ge(drained, 2 * G0["odd_q0"])

            def odd(kind, g):
                ph = f"odd_{kind}{g}"
                W, ki = odd_at(ph), "qkv".index(kind)
                f0 = ki * 0 + g * D

                def body(it, last):
                    for s in range(2):
                        if kind != "q":
                            b = it * 2 + (s + (0 if kind == "k" else 4))
                            wait(pool, unit1_done, it * 2 + (W - 12 + s - 1))
                            src = a[f"dil{g}_k"][bass.ds(b, 1)].rearrange("o (i r) f -> i (o r) f", r=DIL[g])
                            n = NT if g else 1
                            pool.dma_start(u1_k[:, s, 0:n], src[:, 0:n]).then_inc(u1_in[s], 16)
                            rows = scratch["rows1"][0][bass.ds(b * NT, NT), g * D:(g + 1) * D].rearrange("t (o f) -> o t f", o=1)
                            pool.dma_start(u1_q[s][:], rows.to_broadcast([P, NT, D])).then_inc(u1_in[s], 16)
                        if kind != "v":
                            dst = scratch["q1"] if kind == "q" else k1
                            for c in range(2):
                                n = 2 * s + c
                                pool.wait_ge(drained, it * 4 + (2 * G0[ph] + n + 1))
                                pool.dma_start(dst[bass.ds(it * 4 + (8 * g + n), 1)].rearrange("o p n -> p (o n)"),
                                               stage1[:, n]).then_inc(st1[n], 16)
                        pool.wait_ge(rows1_done, it * 2 + (W + s + 1))
                        pool.dma_start(scratch["rows1"][ki][:, bass.ds(it * 512 + (g * D + s * 256), 256)],
                                       row1[:, s]).then_inc(row_stored[s], 16)
                        if kind == "v":
                            pool.wait_ge(v1_done, it * 2 + (4 * g + s + 1))
                            pool.dma_start(v1[g].rearrange("(t p) f -> p t f", p=P)[:, :, bass.ds(it * 512 + s * 256, 256)],
                                           v_row1[:]).then_inc(v1_stored, 16)
                if ph == "odd_k0":
                    for n in range(2):
                        pool.wait_ge(row_stored[n], 16 * 6)
                turns(pool, 2, body, peel_first=(ph == "odd_k0"))
            for kind, g in ODD:
                odd(kind, g)
            projection_stored(pool)
            for ki, kind in ((1, "k"), (2, "v")):
                for g in range(3):
                    pool.dma_start(o[f"dil{g}_{kind}s"][:, N_PAST[g] - NT:N_PAST[g]],
                                   scratch["rows1"][ki][:, g * D:(g + 1) * D].rearrange("(b t) f -> b t f", t=NT)).then_inc(out_done, 16)
            for call in (1, 2, 3):
                attention_stores(call)
            sample_stores(1)
            pool.wait_ge(out_done, 16 * 25)
            pool.wait_ge(h_out, 16 * NG_SSM)
            pool.wait_ge(hs_out, 16 * NG_SSM)


def _feature_major(x):
    n, f = x.shape
    return np.ascontiguousarray(x.T.reshape(f // P, P, n).transpose(1, 0, 2))


def _consts(g):
    l, s = np.arange(P)[None, :], np.arange(P)[:, None]
    bl, bs = l[:, :NS] // NT, s[:NS] // NT
    ls, ss = l[:, :NS], s[:NS]
    v = {
        "tri": s <= l, "neg": np.where(s <= l, 0.0, NEG),
        "tri_s": (ss <= ls) & (bl == bs), "neg_s": np.where((ss <= ls) & (bl == bs), 0.0, NEG),
        "ones_s": bl == bs, "bmask": bs == np.arange(NB)[None, :],
        "sink": g["even_sinks"][0][:, None], "dt_bias": g["even_dt_bias"][0][:, None], "a_log": g["even_a_log"][0][:, None],
        "d_skip": np.repeat(g["even_d_skip"][0], HP).reshape(16, P).T,
        "ssm_norm": g["even_ssm_norm"][0].reshape(16, P).T,
    }
    out, at = np.zeros((P, N_CONSTS), np.float32), 0
    for name, rows, w in CONSTS:
        out[:rows, at:at + w] = v[name]
        at += w
    return out


def _at_consts():
    far = 1.0e30
    q, k = np.arange(P)[:, None], np.arange(P)[None, :]
    own = np.where(k <= q, q - k, far)
    prev = np.where(k >= q, q + P - k, far)
    dist2 = np.where((q // 32 == k // 32) & (k <= q), q - k, far)
    slopes = 2.0 ** (-8.0 * np.arange(1, 17) / 16)
    dil = np.array([1, 1, 4, 16])
    bt, row = np.arange(P) % NS, np.arange(P) // NS
    t, i = (bt % NT)[:, None], np.arange(P)[None, :]
    bt2 = np.arange(NS)[None, :]
    same = (bt // NT)[:, None] == bt2 // NT
    t2 = bt2 % NT
    v = {
        "dist0": np.hstack([own] + [prev, own] * 3), "dist1": own, "dist2": dist2,
        "slope": np.tile(-(slopes[None, :] * dil[:, None]).reshape(1, 64), (P, 1)),
        "sdist0": np.hstack([np.where(i >= t, P + t - i, far), np.where(same & (t2 <= t), t - t2, far)]),
        "sdist1": np.hstack([P - i + 0 * t, np.where(same & (t2 == t), 0, far)]),
        "sslope": -np.stack([slopes[hb * 4 + row] * d for d in dil for hb in range(4)], axis=1),
    }
    return np.hstack([v[n] for n, _ in AT_CONSTS]).astype(np.float32)


def _arrays(i):
    g = {k: np.asarray(v) for k, v in i.items()}
    x = np.concatenate([g["x_prompt"].reshape(SEQ, D), g["x_sample"].reshape(NS, D)])
    cols = lambda v: v.reshape(-1, P).T
    m = {
        "x_t": _feature_major(x),
        "norm_w": np.stack([cols(g["norm_mix"][0]), cols(g["norm_mlp"][0]), cols(g["norm_mix"][1]),
                            cols(g["norm_mlp"][1]), cols(g["final_norm"])], axis=1),
        "conv_wb": np.stack([cols(w) for w in (*g["even_conv_w"][0], g["even_conv_b"][0])], axis=2),
        "conv_state": g["state_conv"][0].transpose(2, 0, 1).reshape(XC, P, NB * 3).transpose(1, 0, 2),
        "ident": np.eye(P, dtype=np.float32),
        "even_w_in": g["even_w_in"][0],
        "h0": g["state_ssm"][0].reshape(NB, NG_SSM, 8 * HP, DS).transpose(1, 3, 0, 2),
        "swa_k": g["cache_swa_k"][0].reshape(NB, P, P), "swa_v": g["cache_swa_v"][0].reshape(NB, P, P),
        "even_w_out": g["even_w_out"][0],
        "w_up0": g["w_up"][0], "w_down0": g["w_down"][0], "w_up1": g["w_up"][1], "w_down1": g["w_down"][1],
        "odd_w_in": g["odd_w_in"][0], "odd_w_out": g["odd_w_out"][0],
        **{f"dil{n}_{k}": g[f"cache_dil{n}_{k}"][0].reshape(NB, N_PAST[n], D) for n in range(3) for k in "kv"},
        "consts": _consts(g), "at_c": _at_consts(),
    }
    return {k: np.ascontiguousarray(v) for k, v in m.items()}


_OUTS = {
    "y": (P, KC, R), "k1": (24, P, R), "v1": (3, SEQ, D),
    **{f"dil{n}_{k}s": (NB, N_PAST[n], D) for n in range(3) for k in "kv"},
    "conv": (P, XC, 27), "ssm_p": (NG_SSM, DS, 8 * HP), "ssm_s": (NG_SSM, DS, NB, 8 * HP),
    "swa_kp": (P, P), "swa_vp": (P, P), "swa_ks": (NB, P, P), "swa_vs": (NB, P, P),
}
_SCRATCH = {
    "q0": (8, P, R), "k0": (P, R), "v0": (SEQ, P), "z0": (16, P, R), "q_row0": (NS, D), "a_row": (32, R), "stats": (4, 128, P), "stats_s": (2, 64, NS), "fac": (3, 16, R), "vn0": (NS, P), "q1": (24, P, R), "rows1": (3, NS, 3 * D),
}


def _returned(r):
    def rows(x):
        return np.ascontiguousarray(x.T)
    conv = r["conv"].transpose(2, 1, 0).reshape(27, CONV_DIM)
    y = r["y"].transpose(2, 1, 0).reshape(R, D)
    out = [y[:SEQ].reshape(1, SEQ, D), y[SEQ:].reshape(NB, NT, D)]
    kv = (2, HEAD_DIM)
    out += [rows(r["swa_kp"]).reshape(1, 1, P, *kv), r["swa_ks"].reshape(1, NB, P, *kv),
            r["swa_vp"].reshape(1, 1, P, *kv), r["swa_vs"].reshape(1, NB, P, *kv)]
    out += [conv[:3].reshape(1, 1, 3, CONV_DIM), conv[3:].reshape(NB, 3, CONV_DIM)[None]]
    out += [r["ssm_p"].transpose(0, 2, 1).reshape(1, 1, NH_SSM, HP, DS),
            r["ssm_s"].transpose(2, 0, 3, 1).reshape(1, NB, NH_SSM, HP, DS)]
    for g, d in enumerate(DIL):
        keep = min(N_PAST[g], SEQ)
        k = r["k1"][8 * g:8 * g + 8, :, :SEQ].reshape(D, d, SEQ // d).transpose(2, 1, 0).reshape(SEQ, D)
        v = r["v1"][g].reshape(d, SEQ // d, D).transpose(1, 0, 2).reshape(SEQ, D)
        for x, nm in ((k, f"dil{g}_ks"), (v, f"dil{g}_vs")):
            out += [x[SEQ - keep:].reshape(1, 1, keep, 16, HEAD_DIM), r[nm].reshape(1, NB, N_PAST[g], 16, HEAD_DIM)]
    return tuple(np.ascontiguousarray(x) for x in out)


def kernel(**inputs):
    import concourse.bacc as _bacc
    from concourse.bass_utils import run_bass_kernel_spmd as _run

    arrays = _arrays(inputs)
    nc = _bacc.Bacc("TRN2", target_bir_lowering=False, num_devices=1)
    a = {k: nc.dram_tensor("in_" + k, v.shape, F32, kind="ExternalInput").ap() for k, v in arrays.items()}
    o = {k: nc.dram_tensor("out_" + k, v, F32, kind="ExternalOutput").ap() for k, v in _OUTS.items()}
    s = {k: nc.dram_tensor("tmp_" + k, v, F32).ap() for k, v in _SCRATCH.items()}
    build(nc, a, o, s)
    r = _run(nc, [{"in_" + k: v for k, v in arrays.items()}], core_ids=[0])
    return _returned({k: r.results[0]["out_" + k] for k in _OUTS})
```
